# Optimizing a Trainium2 kernel written in Bass

```python
import jax, jax.numpy as jnp
from jax import lax
import numpy as np

D_MODEL = 1024
BATCH = 1
SEQ = 1024
DEPTH = 1
DEC_BATCH = 8
DEC_SEQ = 1
PAST_LEN = 8192
PAGE_SIZE = 128

N_META = 16
D_A = D_MODEL
D_B = D_MODEL
CONV_A = 31
CONV_B = 3
BUF_A = min(CONV_A - 1, PAST_LEN)
BUF_B = min(CONV_B - 1, PAST_LEN)
RMS_EPS = 1e-6
LN_EPS = 1e-5

D_IN = 3 * D_A + 4 * D_B + 2 * D_MODEL
SPLIT_IDX = (
    D_A,
    2 * D_A,
    3 * D_A,
    3 * D_A + D_B,
    3 * D_A + 2 * D_B,
    3 * D_A + 3 * D_B,
    3 * D_A + 4 * D_B,
    3 * D_A + 4 * D_B + D_MODEL,
)

kernel_name = "hybrid_conformer_shortconv_gated_decoder_step"

def rmsnorm(x, g):
    xf = x.astype(jnp.float32)
    y = xf * lax.rsqrt(jnp.mean(xf * xf, axis=-1, keepdims=True) + RMS_EPS)
    return (y * g.astype(jnp.float32)).astype(x.dtype)

def layernorm(x, g, b):
    xf = x.astype(jnp.float32)
    mu = jnp.mean(xf, axis=-1, keepdims=True)
    xc = xf - mu
    var = jnp.mean(xc * xc, axis=-1, keepdims=True)
    y = xc * lax.rsqrt(var + LN_EPS)
    return (y * g.astype(jnp.float32) + b.astype(jnp.float32)).astype(x.dtype)

def causal_dwconv(buf, u, w):
    pad = jnp.concatenate([buf.astype(u.dtype), u], axis=1)
    c = u.shape[-1]
    out = lax.conv_general_dilated(
        pad, w.astype(u.dtype)[:, None, :],
        window_strides=(1,), padding='VALID',
        dimension_numbers=('NWC', 'WIO', 'NWC'),
        feature_group_count=c)
    new_buf = pad[:, pad.shape[1] - buf.shape[1]:, :]
    return out, new_buf

def mixer_layer(h, buf_a, buf_b, norm_g, w_in, conv_a_w, conv_a_b, ln_a_g, ln_a_b,
                conv_b_w, w_pa, w_pb, w_out):
    z = rmsnorm(h, norm_g)
    proj = jnp.einsum('btd,de->bte', z, w_in)
    a_val, a_glu, a_gate, b_h, b_c, b_b, b_gate, m_a, m_b = jnp.split(proj, SPLIT_IDX, axis=-1)
    u_a = a_val * jax.nn.sigmoid(a_glu)
    c_a, new_buf_a = causal_dwconv(buf_a, u_a, conv_a_w)
    c_a = layernorm(c_a + conv_a_b.astype(c_a.dtype), ln_a_g, ln_a_b)
    y_a = jax.nn.silu(c_a) * jax.nn.silu(a_gate)
    u_b = b_c * b_h
    c_b, new_buf_b = causal_dwconv(buf_b, u_b, conv_b_w)
    y_b = b_b * c_b * jax.nn.silu(b_gate)
    merged = (jax.nn.sigmoid(m_a) * jnp.einsum('btc,cd->btd', y_a, w_pa)
              + jax.nn.sigmoid(m_b) * jnp.einsum('btc,cd->btd', y_b, w_pb))
    h = h + jnp.einsum('btd,de->bte', merged, w_out)
    return h, new_buf_a, new_buf_b

def setup_inputs(seed: int = 0) -> dict:
    key = jax.random.key(seed)
    ks = jax.random.split(key, 18)
    f32 = jnp.float32
    x_prompt = jax.random.normal(ks[0], (BATCH, SEQ, D_MODEL), f32)
    x_sample = jax.random.normal(ks[1], (DEC_BATCH, DEC_SEQ, D_MODEL), f32)
    state_conv_a = 0.5 * jax.random.normal(ks[2], (DEPTH, DEC_BATCH, BUF_A, D_A), f32)
    state_conv_b = 0.5 * jax.random.normal(ks[3], (DEPTH, DEC_BATCH, BUF_B, D_B), f32)
    meta_tokens = jax.random.normal(ks[4], (N_META, D_MODEL), f32)
    norm_g = 1.0 + 0.02 * jax.random.normal(ks[5], (DEPTH, D_MODEL), f32)
    w_in = jax.random.normal(ks[6], (DEPTH, D_MODEL, D_IN), f32) * D_MODEL ** -0.5
    conv_a_w = jax.random.normal(ks[7], (DEPTH, CONV_A, D_A), f32) * CONV_A ** -0.5
    conv_a_b = 0.02 * jax.random.normal(ks[8], (DEPTH, D_A), f32)
    ln_a_g = 1.0 + 0.02 * jax.random.normal(ks[9], (DEPTH, D_A), f32)
    ln_a_b = 0.02 * jax.random.normal(ks[10], (DEPTH, D_A), f32)
    conv_b_w = jax.random.normal(ks[11], (DEPTH, CONV_B, D_B), f32) * CONV_B ** -0.5
    w_pa = jax.random.normal(ks[12], (DEPTH, D_A, D_MODEL), f32) * D_A ** -0.5
    w_pb = jax.random.normal(ks[13], (DEPTH, D_B, D_MODEL), f32) * D_B ** -0.5
    w_out = jax.random.normal(ks[14], (DEPTH, D_MODEL, D_MODEL), f32) * D_MODEL ** -0.5
    final_norm_g = 1.0 + 0.02 * jax.random.normal(ks[15], (D_MODEL,), f32)
    return {
        "x_prompt": x_prompt, "x_sample": x_sample,
        "state_conv_a": state_conv_a, "state_conv_b": state_conv_b,
        "meta_tokens": meta_tokens, "norm_g": norm_g, "w_in": w_in,
        "conv_a_w": conv_a_w, "conv_a_b": conv_a_b, "ln_a_g": ln_a_g, "ln_a_b": ln_a_b,
        "conv_b_w": conv_b_w, "w_pa": w_pa, "w_pb": w_pb, "w_out": w_out,
        "final_norm_g": final_norm_g,
    }

def reference(x_prompt, x_sample, state_conv_a, state_conv_b, meta_tokens, norm_g, w_in,
              conv_a_w, conv_a_b, ln_a_g, ln_a_b, conv_b_w, w_pa, w_pb, w_out, final_norm_g):
    n_p = x_prompt.shape[0]
    meta = jnp.broadcast_to(meta_tokens.astype(x_prompt.dtype)[None], (n_p, N_META, D_MODEL))
    h_p = jnp.concatenate([meta, x_prompt], axis=1)
    h_s = x_sample
    new_a_p, new_b_p, new_a_s, new_b_s = [], [], [], []
    for l in range(DEPTH):
        lw = (norm_g[l], w_in[l], conv_a_w[l], conv_a_b[l], ln_a_g[l], ln_a_b[l],
              conv_b_w[l], w_pa[l], w_pb[l], w_out[l])
        zero_a = jnp.zeros((n_p, BUF_A, D_A), h_p.dtype)
        zero_b = jnp.zeros((n_p, BUF_B, D_B), h_p.dtype)
        h_p, ba_p, bb_p = mixer_layer(h_p, zero_a, zero_b, *lw)
        h_s, ba_s, bb_s = mixer_layer(h_s, state_conv_a[l], state_conv_b[l], *lw)
        new_a_p.append(ba_p)
        new_b_p.append(bb_p)
        new_a_s.append(ba_s)
        new_b_s.append(bb_s)
    y_prompt = rmsnorm(h_p, final_norm_g)[:, N_META:, :]
    y_sample = rmsnorm(h_s, final_norm_g)
    new_conv_a_prompt = jnp.stack(new_a_p, axis=0)
    new_conv_b_prompt = jnp.stack(new_b_p, axis=0)
    new_conv_a_sample = jnp.stack(new_a_s, axis=0)
    new_conv_b_sample = jnp.stack(new_b_s, axis=0)
    return (y_prompt, y_sample, new_conv_a_prompt, new_conv_b_prompt, new_conv_a_sample, new_conv_b_sample)


_drawn_inputs = setup_inputs


def setup_inputs(seed=0):
    import zlib

    import numpy as np

    out = dict(_drawn_inputs(seed))
    spreads = {}
    factors = {'conv_a_b': 7.456, 'ln_a_g': 8.0, 'ln_a_b': 8.0, 'final_norm_g': 2.819}
    for name, (base, spread) in spreads.items():
        noise = np.random.default_rng([zlib.crc32(name.encode()), seed]).standard_normal(out[name].shape)
        drawn = base * np.exp(spread * noise) if base else spread * noise
        out[name] = __import__('jax').numpy.asarray(drawn.astype(out[name].dtype))
    for name, factor in factors.items():
        out[name] = (out[name] * factor).astype(out[name].dtype)
    return out
```

```python
from contextlib import ExitStack

import concourse.bass as bass
from concourse import mybir
from concourse.alu_op_type import AluOpType as ALU

ACT = mybir.ActivationFunctionType
F32 = mybir.dt.float32
F32R = mybir.dt.float32r

P = 128
RMS_EPS, LN_EPS = 1e-6, 1e-5


def wait(eng, sem, value):
    if not isinstance(value, int) or value > 0:
        eng.wait_ge(sem, value)


def decoder_step(nc, x_prompt, x_sample, state_conv_a, state_conv_b, meta_tokens, norm_g, w_in, conv_a_w,
                 conv_a_b, ln_a_g, ln_a_b, conv_b_w, w_pa, w_pb, w_out, final_norm_g,
                 y_prompt, y_sample, new_a_prompt, new_b_prompt, new_a_sample, new_b_sample):
    _, SEQ, D = x_prompt.shape
    DEC = x_sample.shape[0]
    META = meta_tokens.shape[0]
    TAPS_A, TAPS_B = conv_a_w.shape[1], conv_b_w.shape[1]
    BUF_A, BUF_B = TAPS_A - 1, TAPS_B - 1
    K = D // P
    TOK = SEQ + DEC
    ALL = META + TOK
    CHUNKS = 3
    CW = TOK // CHUNKS
    CWM = CW + 6
    ZT = CHUNKS * CWM
    CWB = CW + 2
    SKIP = ZT - CHUNKS * CWB
    assert D == 1024 and SEQ == 1024 and DEC == 8 and META == 16 and CW * CHUNKS == TOK and ZT >= ALL and SKIP <= META - BUF_B
    HALF = SEQ // 2
    LEAD = BUF_A - META
    UA_S = BUF_A + SEQ
    UB_S = META + SEQ - SKIP
    TAIL_A, TAIL_B = BUF_A + DEC, BUF_B + DEC
    TAIL = TAIL_A + TAIL_B
    A_VAL, A_GLU, A_GATE, B_H, B_C, B_B, B_GATE, M_A, M_B = (D * i for i in range(9))
    PH1 = [(A_GLU, 0, CWM), (A_VAL, 0, CWM), (B_H, SKIP, CWB), (B_C, SKIP, CWB), (B_B, META, CW), (B_GATE, META, CW)]
    N1, N2, N3, N4 = len(PH1) * K, 2 * K, 2 * K, K
    I2, I3, I4, I5 = N1, N1 + N2, N1 + N2 + N3, N1 + N2 + N3 + N4
    TT = (TOK + P - 1) // P
    XT = (ALL + P - 1) // P
    LAST5, LASTX = TOK - P * (TT - 1), ALL - P * (XT - 1)
    CONV_OPS = 2 * TAPS_A
    CONSTS = TAPS_A + TAPS_B + 3
    C_TB, C_BIAS, C_LNG, C_LNB = TAPS_A, TAPS_A + TAPS_B, TAPS_A + TAPS_B + 1, TAPS_A + TAPS_B + 2

    spill = nc.dram_tensor("merged_b_spill", [P, K, TOK], F32).ap()

    with ExitStack() as ctx:
        def sb(name, shape, dt=F32):
            return ctx.enter_context(nc.sbuf_tensor(name, shape, dt))

        def pb(name, shape):
            return ctx.enter_context(nc.psum_tensor(name, shape, F32))

        def sem(name):
            return ctx.enter_context(nc.semaphore(name))

        z_hi = sb("z_hi", [P, K, ZT], F32R)
        z_lo = sb("z_lo", [P, K, ZT], F32R)
        y_hi = sb("y_hi", [P, K, TOK], F32R)
        y_lo = sb("y_lo", [P, K, TOK], F32R)
        c = sb("c", [P, K, TOK])
        w_hi = sb("w_hi", [P, 2, K, P], F32R)
        w_lo = sb("w_lo", [P, 2, K, P], F32R)
        raw = sb("raw", [P, 2, K, P])
        t1 = sb("t1", [P, ZT])
        t2 = sb("t2", [P, ZT])
        ua = sb("ua", [P, LEAD + ZT])
        sq = sb("sq", [P, TOK])
        st_raw = sb("st_raw", [P, 2, P])
        sa = sb("sa", [P, DEC, TAPS_A])
        sbw = sb("sbw", [P, DEC, TAPS_B])
        tail_in = sb("tail_in", [P, P])
        tail_out = sb("tail_out", [TAIL, P])
        cst = sb("cst", [P, K, CONSTS])
        ident = sb("ident", [P, P])
        ssum = sb("ssum", [P, 2 * XT])
        root = sb("root", [P, 2 * XT])
        rinv = sb("rinv", [P, 2 * XT])
        eps = sb("eps", [P, 2])
        gfin = ua[:, 0:D]

        w_out_hi = z_hi[:, :, :].rearrange("p k t -> p (k t)")[:, 0:K * D].rearrange("p (k e) -> p k e", k=K)
        w_out_lo = z_lo[:, :, :].rearrange("p k t -> p (k t)")[:, 0:K * D].rearrange("p (k e) -> p k e", k=K)

        ps = [pb("ps0", [P, CHUNKS, 512]), pb("ps1", [P, CHUNKS, 512])]
        spare = [pb("spare0", [P, 512]), pb("spare1", [P, 512])]

        x_in = [sem(f"x_in{i}") for i in range(XT)]
        gin_in, cst_in, raw_in = sem("gin_in"), sem("cst_in"), [sem("raw_in0"), sem("raw_in1")]
        pool_const = sem("pool_const")
        sq_done, root_done, xn_ready, rinv_done = sem("sq_done"), sem("root_done"), sem("xn_ready"), sem("rinv_done")
        xt_done, zhi_done, zlo_done = sem("xt_done"), sem("zhi_done"), sem("zlo_done")
        cst_t, cst_ready = sem("cst_t"), sem("cst_ready")
        hi_ready, lo_ready = sem("hi_ready"), sem("lo_ready")
        chunk_done = sem("chunk_done")
        glu_ready, ua_ready, bh_ready, ub_ready, bsig_ready = (
            sem("glu_ready"), sem("ua_ready"), sem("bh_ready"), sem("ub_ready"), sem("bsig_ready"))
        conv_step, cb_step, samp_step, yb_step = sem("conv_step"), sem("cb_step"), sem("samp_step"), sem("yb_step")
        yhi_ready, ylo_ready = sem("yhi_ready"), sem("ylo_ready")
        st_in, st_t, sa_in, sb_in = sem("st_in"), sem("st_t"), sem("sa_in"), sem("sb_in")
        tail_ready, tail_t, tail_rows, tail_stored = sem("tail_ready"), sem("tail_t"), sem("tail_rows"), sem("tail_stored")
        mb_ready, mbp_ready, spilled = sem("mb_ready"), sem("mbp_ready"), sem("spilled")
        sum_step, mean_t, mean_ready, sub_done = sem("sum_step"), sem("mean_t"), sem("mean_ready"), sem("sub_done")
        sqr_ready, sqacc_step, var_t, std_ready, rstd_ready, ln_done = (
            sem("sqr_ready"), sem("sqacc_step"), sem("var_t"), sem("std_ready"), sem("rstd_ready"), sem("ln_done"))
        asig_ready, nsig_ready, ya_step, ahi_ready, alo_ready, ma_ready = (
            sem("asig_ready"), sem("nsig_ready"), sem("ya_step"), sem("ahi_ready"), sem("alo_ready"), sem("ma_ready"))
        mb_back, mul_done, merged_done = [sem("mb_back0"), sem("mb_back1")], sem("mul_done"), sem("merged_done")
        out_mm, xr_in, gf_in = sem("out_mm"), [sem("xr_in0"), sem("xr_in1")], sem("gf_in")
        h_ready, hsq_done, hroot_done, hinv_done, y_ready = (
            sem("h_ready"), sem("hsq_done"), sem("hroot_done"), sem("hinv_done"), sem("y_ready"))
        y_stored, copied = [sem("y_stored0"), sem("y_stored1")], sem("copied")

        def at(tensor, j):
            if isinstance(j, int):
                return tensor[:, j, :]
            return tensor[:, bass.ds(j, 1), :].rearrange("p a n -> p (a n)")

        def const(j, i, n=1):
            if isinstance(j, int):
                return cst[:, j, i:i + n]
            return cst[:, bass.ds(j, 1), i:i + n].rearrange("p a n -> p (a n)")

        def f(ap):
            return ap.bitcast(F32)

        def item_psum(s, width):
            return ps[s][:, :, 0:width]

        def chunked(ap, width):
            return ap.rearrange("p (c w) -> p c w", w=width)

        def item_end(n):
            if isinstance(n, int) and n == 0:
                return 2 * CHUNKS - 1
            return (n + 1) * CHUNKS

        def x_slot(i):
            return c[:, i, 0:D] if i < K - 1 else (t1 if i == K - 1 else t2)[:, 0:D]

        def x_bank(i, h):
            return spare[h][:, :] if i % 2 == 0 else ps[1][:, 1 + h, :]

        gin = c[:, K - 1, 0:D]

        def x_rows(i):
            return P if i < XT - 1 else LASTX

        def w_src(w, col):
            if isinstance(col, int):
                return w[0, :, col:col + P].rearrange("(k p) e -> p k e", p=P)
            return w[0, :, bass.ds(col, P)].rearrange("(k p) e -> p k e", p=P)

        block = ctx.enter_context(nc.Block())

        @block.sync
        def _(sp):
            def load_item(q, s, w, col):
                src = w_src(w, col)
                wait(sp, lo_ready, q - 1)
                sp.dma_start(raw[:, s, :, :], src).then_inc(raw_in[s], 16)

            def load_x(i):
                dst = x_slot(i)
                if i == 0:
                    sp.dma_start(dst[0:META, :], meta_tokens[:, :]).then_inc(x_in[0], 16)
                    sp.dma_start(dst[META:P, :], x_prompt[0, 0:P - META, :]).then_inc(x_in[0], 16)
                elif i < XT - 1:
                    sp.dma_start(dst[:, :], x_prompt[0, P * i - META:P * (i + 1) - META, :]).then_inc(x_in[i], 16)
                else:
                    n = SEQ - (P * i - META)
                    sp.dma_start(dst[0:n, :], x_prompt[0, P * i - META:SEQ, :]).then_inc(x_in[i], 16)
                    sp.dma_start(dst[n:n + DEC, :], x_sample[:, 0, :]).then_inc(x_in[i], 16)

            for i in range(XT):
                load_x(i)
                if i == 0:
                    sp.dma_start(gin, norm_g[0, :].partition_broadcast(P)).then_inc(gin_in, 16)
                if i == 1:
                    load_item(0, 0, w_in, PH1[0][0])
                if i == 3:
                    load_item(1, 1, w_in, PH1[1][0])
            for src, r0, n in ((conv_a_w[0, :, :], 0, TAPS_A), (conv_b_w[0, :, :], C_TB, TAPS_B),
                               (conv_a_b[0:1, :], C_BIAS, 1), (ln_a_g[0:1, :], C_LNG, 1), (ln_a_b[0:1, :], C_LNB, 1)):
                sp.dma_start(sq[r0:r0 + n, 0:D], src).then_inc(cst_in, 16)

            def phase1(j, first=0):
                wait(sp, st_t, 2 * j)
                cols = slice(P * j, P * (j + 1)) if isinstance(j, int) else bass.ds(P * j, P)
                sp.dma_start(st_raw[0:4 * BUF_A, :, :],
                             state_conv_a[0, :, :, cols].rearrange("(h b) r e -> (b r) h e", h=2)).then_inc(st_in, 16)
                sp.dma_start(st_raw[4 * BUF_A:4 * (BUF_A + BUF_B), :, :],
                             state_conv_b[0, :, :, cols].rearrange("(h b) r e -> (b r) h e", h=2)).then_inc(st_in, 16)
                for s, (col, _, _) in enumerate(PH1):
                    if s < first:
                        continue
                    load_item(j * len(PH1) + s, s % 2, w_in, j * P + col)
                    if s == 3 and not (isinstance(j, int) and j == 0):
                        store_tails(j - 1)

            def store_tails(j):
                wait(sp, tail_rows, j + 1)
                cols = slice(P * j, P * (j + 1)) if isinstance(j, int) else bass.ds(P * j, P)
                for dst, r0, n in ((new_a_prompt[0, 0, :, cols], 0, BUF_A),
                                   (new_a_sample[0, :, BUF_A - 1, cols], BUF_A, DEC),
                                   (new_b_prompt[0, 0, :, cols], TAIL_A, BUF_B),
                                   (new_b_sample[0, :, BUF_B - 1, cols], TAIL_A + BUF_B, DEC)):
                    sp.dma_start(dst, tail_out[r0:r0 + n, :]).then_inc(tail_stored, 16)

            phase1(0, first=2)
            with sp.Fori(1, K) as j:
                phase1(j)

            def phase2(j):
                load_item(I2 + 2 * j, 0, w_in, j * P + M_B)
                load_item(I2 + 2 * j + 1, 1, w_pb, (j + 1) * P - P)
                if not (isinstance(j, int) and j == 0):
                    spill_out(j - 1)

            def spill_out(j):
                wait(sp, mbp_ready, j + 1)
                dst = spill[:, j, :] if isinstance(j, int) else spill[:, bass.ds(j, 1), :].rearrange("p a n -> p (a n)")
                sp.dma_start(dst, t2[:, 0:TOK]).then_inc(spilled, 16)

            phase2(0)
            phase2(1)
            store_tails(K - 1)
            sp.dma_start(new_a_sample[0, :, 0:BUF_A - 1, :], state_conv_a[0, :, 1:BUF_A, :]).then_inc(copied, 16)
            sp.dma_start(new_b_sample[0, :, 0:BUF_B - 1, :], state_conv_b[0, :, 1:BUF_B, :]).then_inc(copied, 16)
            with sp.Fori(2, K) as j:
                phase2(j)

            def phase3(j):
                load_item(I3 + 2 * j, 0, w_in, j * P + A_GATE)
                load_item(I3 + 2 * j + 1, 1, w_in, j * P + M_A)

            phase3(0)
            spill_out(K - 1)
            with sp.Fori(1, K) as j:
                phase3(j)

            def load_back(j, s):
                t = (t1, t2)[s]
                if isinstance(j, int) and j < 2:
                    wait(sp, alo_ready, K)
                    wait(sp, spilled, 16 * K)
                else:
                    wait(sp, merged_done, CHUNKS * (j - 1))
                src = spill[:, j, :] if isinstance(j, int) else spill[:, bass.ds(j, 1), :].rearrange("p a n -> p (a n)")
                sp.dma_start(t[:, 0:TOK], src).then_inc(mb_back[s], 16)

            def load_out_rows(q, s, m):
                wait(sp, lo_ready, q - 1)
                rows = slice(P * m, P * (m + 1)) if isinstance(m, int) else bass.ds(P * m, P)
                sp.dma_start(raw[:, s, :, :].rearrange("p k e -> p (k e)"), w_out[0, rows, :]).then_inc(raw_in[s], 16)

            load_item(I4, 0, w_pa, 0)
            load_item(I4 + 1, 1, w_pa, P)
            load_back(0, 0)
            load_back(1, 1)

            def phase4(m, s):
                load_out_rows(I4 + 2 + 2 * m, 0, m)
                load_item(I4 + 3 + 2 * m, 1, w_pa, m * P + 2 * P)
                load_back(m + 2, s)

            phase4(0, 0)
            phase4(1, 1)
            with sp.Fori(1, (K - 2) // 2) as jj:
                phase4(2 * jj, 0)
                phase4(2 * jj + 1, 1)
            load_out_rows(I4 + 2 * K - 2, 0, K - 2)
            load_out_rows(I4 + 2 * K - 1, 1, K - 1)

            wait(sp, ln_done, K)
            sp.dma_start(gfin, final_norm_g.partition_broadcast(P)).then_inc(gf_in, 16)

            def load_res(i, s):
                if isinstance(i, int) and i < 2:
                    wait(sp, merged_done, CHUNKS * (K - 1 + i))
                else:
                    wait(sp, y_stored[s], 8 * (i - s))
                t = (t1, t2)[s]
                if isinstance(i, int) and i == TT - 1:
                    sp.dma_start(t[0:DEC, 0:D], x_sample[:, 0, :]).then_inc(xr_in[s], 16)
                else:
                    rows = slice(P * i, P * (i + 1)) if isinstance(i, int) else bass.ds(P * i, P)
                    sp.dma_start(t[:, 0:D], x_prompt[0, rows, :]).then_inc(xr_in[s], 16)

            def store_y(i, s):
                wait(sp, y_ready, i + 1)
                t = (t1, t2)[s]
                if isinstance(i, int) and i == TT - 1:
                    sp.dma_start(y_sample[:, 0, :], t[0:DEC, 0:D]).then_inc(y_stored[s], 16)
                else:
                    rows = slice(P * i, P * (i + 1)) if isinstance(i, int) else bass.ds(P * i, P)
                    sp.dma_start(y_prompt[0, rows, :], t[:, 0:D]).then_inc(y_stored[s], 16)

            load_res(0, 0)
            load_res(1, 1)
            with sp.Fori(0, (TT - 1) // 2 - 1) as ii:
                for s in range(2):
                    store_y(2 * ii + s, s)
                    load_res(2 * ii + s + 2, s)
            store_y(TT - 3, 0)
            load_res(TT - 1, 0)
            store_y(TT - 2, 1)
            store_y(TT - 1, 0)
            sp.wait_ge(y_stored[0], 16 * ((TT + 1) // 2))
            sp.wait_ge(y_stored[1], 16 * (TT // 2))
            sp.wait_ge(tail_stored, 64 * K)
            sp.wait_ge(copied, 32)
            sp.wait_ge(spilled, 16 * K)

        @block.gpsimd
        def _(pool):
            nc.gpsimd.memset(eps[:, 0:1], RMS_EPS)
            nc.gpsimd.memset(eps[:, 1:2], LN_EPS).then_inc(pool_const, 1)
            nc.gpsimd.memset(ident[:, :], 0.0).then_inc(pool_const, 1)
            pool.wait_ge(pool_const, 2)
            nc.gpsimd.affine_select(out=ident[:, :], in_=ident[:, :], compare_op=ALU.not_equal, fill=1.0, base=0,
                                    pattern=[[-1, P]], channel_multiplier=1).then_inc(pool_const, 1)
            nc.gpsimd.memset(z_hi[:, :, ALL:ZT].bitcast(F32), 0.0).then_inc(pool_const, 1)
            nc.gpsimd.memset(z_lo[:, :, ALL:ZT].bitcast(F32), 0.0).then_inc(pool_const, 1)
            nc.gpsimd.memset(ua[:, 0:LEAD], 0.0).then_inc(pool_const, 1)
            nc.gpsimd.memset(tail_in[:, :], 0.0).then_inc(pool_const, 1)

            def lo_weights(q, s):
                pool.wait_ge(hi_ready, q + 1)
                nc.gpsimd.tensor_tensor(w_lo[:, s, :, :], raw[:, s, :, :], f(w_hi[:, s, :, :]), ALU.subtract)\
                    .then_inc(lo_ready, 1)

            with pool.Fori(0, I2 // 2 + 1) as qq:
                for s in range(2):
                    lo_weights(2 * qq + s, s)
            pool.wait_ge(tail_t, K)
            nc.gpsimd.memset(ident[:, :], 1.0 / D).then_inc(pool_const, 1)
            with pool.Fori(I2 // 2 + 1, I4 // 2 + 1) as qq:
                for s in range(2):
                    lo_weights(2 * qq + s, s)

            def lo_out_rows(q, s, m):
                pool.wait_ge(hi_ready, q + 1)
                nc.gpsimd.tensor_tensor(at(w_out_lo, m), raw[:, s, :, :].rearrange("p k e -> p (k e)"),
                                        f(at(w_out_hi, m)), ALU.subtract).then_inc(lo_ready, 1)

            def lo_pa(q, ring):
                pool.wait_ge(hi_ready, q + 1)
                nc.gpsimd.tensor_tensor(w_lo[:, ring, :, :], raw[:, 1, :, :], f(w_hi[:, ring, :, :]), ALU.subtract)\
                    .then_inc(lo_ready, 1)

            with pool.Fori(0, (K - 2) // 2) as jj:
                for r in range(2):
                    lo_out_rows(I4 + 2 + 2 * r + 4 * jj, 0, 2 * jj + r)
                    lo_pa(I4 + 3 + 2 * r + 4 * jj, r)
            lo_out_rows(I4 + 2 * K - 2, 0, K - 2)
            lo_out_rows(I4 + 2 * K - 1, 1, K - 1)

            Q5 = I4 + 2 * K

            def lo_merged(i, s, n=P):
                pool.wait_ge(hi_ready, Q5 + 1 + i)
                cols = slice(P * i, P * i + n) if isinstance(i, int) else bass.ds(P * i, n)
                nc.gpsimd.tensor_tensor(w_lo[:, s, :, 0:n], c[:, :, cols], f(w_hi[:, s, :, 0:n]), ALU.subtract)\
                    .then_inc(lo_ready, 1)

            with pool.Fori(0, (TT - 1) // 2) as ii:
                for s in range(2):
                    lo_merged(2 * ii + s, s)
            lo_merged(TT - 1, 0, LAST5)

        @block.scalar
        def _(act):

            def hi_weights(q, s, item=None):
                act.wait_ge(raw_in[s], (q - s) * 8 + 16)
                item = q if item is None else item
                if not isinstance(item, int) or item >= 2:
                    act.wait_ge(chunk_done, item_end(item - 2))
                nc.scalar.activation(w_hi[:, s, :, :], raw[:, s, :, :], ACT.Copy).then_inc(hi_ready, 1)

            def z_evacuate(i):
                n = x_rows(i)
                for h in range(2):
                    u = 2 * i + h
                    act.wait_ge(xt_done, u + 1)
                    src = x_bank(i, h).rearrange("p (k t) -> p k t", k=4)[:, :, 0:n]
                    nc.scalar.activation(z_hi[:, 4 * h:4 * h + 4, P * i:P * i + n], src, ACT.Copy).then_inc(zhi_done, 1)

            act.wait_ge(pool_const, 1)
            nc.scalar.activation(root[:, 2 * XT - 1:2 * XT], eps[:, 0:1], ACT.Sqrt)
            for i in range(XT):
                n = x_rows(i)
                act.wait_ge(x_in[i], 32 if i in (0, XT - 1) else 16)
                wait(act, sq_done, i)
                nc.scalar.activation(ua[0:n, LEAD + ZT - D:LEAD + ZT], x_slot(i)[0:n, :], ACT.Square,
                                     accum_out=ssum[0:n, i:i + 1]).then_inc(sq_done, 1)
                act.wait_ge(sq_done, i + 1)
                nc.scalar.activation(root[0:n, i:i + 1], ssum[0:n, i:i + 1], ACT.Sqrt, scale=1.0 / D,
                                     bias=eps[0:n, 0:1]).then_inc(root_done, 1)
                if i >= 2:
                    z_evacuate(i - 2)
                if i == 1:
                    hi_weights(0, 0)
                if i == 4:
                    hi_weights(1, 1)
            z_evacuate(XT - 2)
            z_evacuate(XT - 1)
            act.wait_ge(cst_t, 1)
            nc.scalar.activation(cst[:, :, :], spare[0][:, 0:K * CONSTS].rearrange("p (k i) -> p k i", k=K), ACT.Copy)\
                .then_inc(cst_ready, 1)

            def gate_b(j):
                act.wait_ge(chunk_done, (j + 1) * len(PH1) * CHUNKS)
                act.wait_ge(cb_step, 5 * j + 5)
                act.wait_ge(tail_ready, 2 * j + 2)
                nc.scalar.activation(chunked(t2[:, 0:TOK], CW), item_psum(1, CW), ACT.Sigmoid).then_inc(bsig_ready, 1)
                act.wait_ge(yb_step, 3 * j + 3)
                nc.scalar.activation(at(y_hi, j), t1[:, 0:TOK], ACT.Copy).then_inc(yhi_ready, 1)

            def tails_out(j):
                act.wait_ge(tail_t, j + 1)
                wait(act, tail_stored, 64 * j)
                nc.scalar.activation(tail_out[:, :], spare[1][0:TAIL, 0:P], ACT.Copy).then_inc(tail_rows, 1)

            def phase1_act(j):
                n0 = j * len(PH1)
                first = isinstance(j, int) and j == 0
                end = [item_end(n0 + s) for s in range(len(PH1))]
                if not first:
                    hi_weights(n0 + 1, 1)
                    gate_b(j - 1)
                hi_weights(n0 + 2, 0)
                act.wait_ge(chunk_done, end[0])
                wait(act, ylo_ready, j)
                nc.scalar.activation(chunked(t1[:, :], CWM), item_psum(0, CWM), ACT.Sigmoid).then_inc(glu_ready, 1)
                if not first:
                    tails_out(j - 1)
                hi_weights(n0 + 3, 1)
                act.wait_ge(st_t, 2 * j + 2)
                wait(act, samp_step, 3 * j)
                wait(act, cb_step, 5 * j)
                st = spare[0][:, 0:2 * P].rearrange("p (h m) -> p h m", h=2)
                nc.scalar.activation(sa[:, :, 0:BUF_A].rearrange("p (h b) r -> p h b r", h=2),
                                     st[:, :, 0:4 * BUF_A].rearrange("p h (b r) -> p h b r", b=4), ACT.Copy)\
                    .then_inc(sa_in, 1)
                nc.scalar.activation(sbw[:, :, 0:BUF_B].rearrange("p (h b) r -> p h b r", h=2),
                                     st[:, :, 4 * BUF_A:P].rearrange("p h (b r) -> p h b r", b=4), ACT.Copy)\
                    .then_inc(sb_in, 1)
                hi_weights(n0 + 4, 0)
                act.wait_ge(chunk_done, end[2])
                wait(act, yb_step, 3 * j)
                nc.scalar.activation(chunked(t2[:, 0:CHUNKS * CWB], CWB), item_psum(0, CWB), ACT.Copy).then_inc(bh_ready, 1)
                act.wait_ge(ua_ready, j + 1)
                nc.scalar.activation(sa[:, :, BUF_A:TAPS_A], ua[:, UA_S:UA_S + DEC].unsqueeze(2), ACT.Copy)\
                    .then_inc(sa_in, 1)
                wait(act, tail_t, j)
                nc.scalar.activation(tail_in[:, 0:TAIL_A], ua[:, SEQ:SEQ + TAIL_A], ACT.Copy).then_inc(tail_ready, 1)
                hi_weights(n0 + 5, 1)
                hi_weights(n0 + 6, 0)
                act.wait_ge(ub_ready, j + 1)
                nc.scalar.activation(sbw[:, :, BUF_B:TAPS_B], t2[:, UB_S:UB_S + DEC].unsqueeze(2), ACT.Copy)\
                    .then_inc(sb_in, 1)
                nc.scalar.activation(tail_in[:, TAIL_A:TAIL], t2[:, UB_S - BUF_B:UB_S + DEC], ACT.Copy)\
                    .then_inc(tail_ready, 1)

            phase1_act(0)
            with act.Fori(1, K) as j:
                phase1_act(j)

            def sigmoid_mb(j):
                act.wait_ge(chunk_done, item_end(I2 + 2 * j))
                if not isinstance(j, int) or j:
                    act.wait_ge(mbp_ready, j)
                nc.scalar.activation(chunked(t1[:, 0:TOK], CW), item_psum(0, CW), ACT.Sigmoid).then_inc(mb_ready, 1)

            def phase2_act(j):
                hi_weights(I2 + 1 + 2 * j, 1)
                hi_weights(I2 + 2 + 2 * j, 0)
                sigmoid_mb(j)

            def row_of(chunk):
                return ua[:, CW * chunk:CW * (chunk + 1)]

            def stat_bank(chunk):
                return spare[chunk % 2][:, 0:CW]

            def squares(j0, j1):
                for j in range(j0, j1):
                    act.wait_ge(sub_done, j + 1)
                    wait(act, sqacc_step, j)
                    nc.scalar.activation(sq[:, :], c[:, j, :], ACT.Square).then_inc(sqr_ready, 1)

            hi_weights(I2 + 1, 1)
            gate_b(K - 1)
            hi_weights(I2 + 2, 0)
            act.wait_ge(ylo_ready, K)
            tails_out(K - 1)
            sigmoid_mb(0)
            phase2_act(1)
            for ch in range(CHUNKS):
                act.wait_ge(mean_t, ch + 1)
                nc.scalar.activation(row_of(ch), stat_bank(ch), ACT.Copy).then_inc(mean_ready, 1)
            hi_weights(I2 + 5, 1)
            squares(0, 2)
            hi_weights(I2 + 6, 0)
            sigmoid_mb(2)
            squares(2, 5)
            hi_weights(I2 + 7, 1)
            squares(5, K)
            hi_weights(I2 + 8, 0)
            sigmoid_mb(3)
            for ch in range(CHUNKS):
                act.wait_ge(var_t, ch + 1)
                nc.scalar.activation(row_of(ch), stat_bank(ch), ACT.Sqrt, bias=eps[:, 1:2]).then_inc(std_ready, 1)
            phase2_act(4)
            with act.Fori(5, K) as j:
                phase2_act(j)

            def gate_m(j):
                act.wait_ge(chunk_done, item_end(I3 + 2 * j + 1))
                act.wait_ge(ya_step, 4 * j + 4)
                nc.scalar.activation(chunked(at(c, j), CW), item_psum(1, CW), ACT.Sigmoid).then_inc(ma_ready, 1)

            def phase3_act(j):
                n0 = I3 + 2 * j
                first = isinstance(j, int) and j == 0
                hi_weights(n0 + 1, 1)
                if first:
                    act.wait_ge(mbp_ready, K)
                    act.wait_ge(spilled, 16 * K)
                    act.wait_ge(ln_done, K)
                else:
                    gate_m(j - 1)
                    act.wait_ge(alo_ready, j)
                nc.scalar.activation(t2[:, 0:TOK], at(c, j), ACT.Sigmoid, scale=const(j, C_LNG),
                                     bias=const(j, C_LNB)).then_inc(nsig_ready, 1)
                hi_weights(n0 + 2, 0)
                act.wait_ge(chunk_done, item_end(n0))
                nc.scalar.activation(chunked(t1[:, 0:TOK], CW), item_psum(0, CW), ACT.Sigmoid).then_inc(asig_ready, 1)
                act.wait_ge(ya_step, 4 * j + 4)
                nc.scalar.activation(at(y_hi, j), t2[:, 0:TOK], ACT.Copy).then_inc(ahi_ready, 1)

            phase3_act(0)
            with act.Fori(1, K) as j:
                phase3_act(j)

            def hi_out_rows(q, s, m):
                act.wait_ge(raw_in[s], (q - s) * 8 + 16)
                act.wait_ge(chunk_done, item_end(I4 - 1))
                nc.scalar.activation(at(w_out_hi, m), raw[:, s, :, :].rearrange("p k e -> p (k e)"), ACT.Copy)\
                    .then_inc(hi_ready, 1)

            def hi_pa(q, ring, item):
                act.wait_ge(raw_in[1], (q - 1) * 8 + 16)
                act.wait_ge(chunk_done, item_end(item - 2))
                nc.scalar.activation(w_hi[:, ring, :, :], raw[:, 1, :, :], ACT.Copy).then_inc(hi_ready, 1)

            hi_weights(I4 + 1, 1)
            gate_m(K - 1)
            with act.Fori(0, (K - 2) // 2) as jj:
                for r in range(2):
                    hi_out_rows(I4 + 2 + 2 * r + 4 * jj, 0, 2 * jj + r)
                    hi_pa(I4 + 3 + 2 * r + 4 * jj, r, I4 + 2 + r + 2 * jj)
            hi_out_rows(I4 + 2 * K - 2, 0, K - 2)
            hi_out_rows(I4 + 2 * K - 1, 1, K - 1)

            def hi_merged(i, s, n=P):
                if isinstance(i, int) and i < 2:
                    act.wait_ge(chunk_done, item_end(I4 + K - 2 + i))
                    act.wait_ge(merged_done, CHUNKS * (K - 1) + 1)
                else:
                    act.wait_ge(out_mm, i - 1)
                    act.wait_ge(merged_done, CHUNKS * K)
                cols = slice(P * i, P * i + n) if isinstance(i, int) else bass.ds(P * i, n)
                nc.scalar.activation(w_hi[:, s, :, 0:n], c[:, :, cols], ACT.Copy).then_inc(hi_ready, 1)

            def final_norm(i, s, n=P):
                col = XT + i if isinstance(i, int) else None
                t = (t1, t2)[s]
                act.wait_ge(h_ready, i + 1)
                act.wait_ge(hsq_done, i) if not isinstance(i, int) or i else None
                a = ssum[0:n, XT + i:XT + i + 1] if col else ssum[0:n, bass.ds(i + XT, 1)]
                b = root[0:n, XT + i:XT + i + 1] if col else root[0:n, bass.ds(i + XT, 1)]
                nc.scalar.activation(sq[0:n, 0:D], t[0:n, 0:D], ACT.Square, accum_out=a).then_inc(hsq_done, 1)
                act.wait_ge(hsq_done, i + 1)
                nc.scalar.activation(b, a, ACT.Sqrt, scale=1.0 / D, bias=eps[0:n, 0:1]).then_inc(hroot_done, 1)

            hi_merged(0, 0)
            hi_merged(1, 1)
            final_norm(0, 0)
            hi_merged(2, 0)
            final_norm(1, 1)
            with act.Fori(1, (TT - 1) // 2 - 1) as ii:
                hi_merged(2 * ii + 1, 1)
                final_norm(2 * ii, 0)
                hi_merged(2 * ii + 2, 0)
                final_norm(2 * ii + 1, 1)
            hi_merged(TT - 2, 1)
            final_norm(TT - 3, 0)
            hi_merged(TT - 1, 0, LAST5)
            final_norm(TT - 2, 1)
            final_norm(TT - 1, 0, LAST5)

        @block.vector
        def _(dve):
            V = nc.vector
            dve.wait_ge(gin_in, 16)

            def z_low(i):
                n = x_rows(i)
                for h in range(2):
                    dve.wait_ge(zhi_done, 2 * i + h + 1)
                    src = x_bank(i, h).rearrange("p (k t) -> p k t", k=4)[:, :, 0:n]
                    V.tensor_tensor(z_lo[:, 4 * h:4 * h + 4, P * i:P * i + n], src,
                                    f(z_hi[:, 4 * h:4 * h + 4, P * i:P * i + n]), ALU.subtract).then_inc(zlo_done, 1)

            for i in range(XT):
                n = x_rows(i)
                dve.wait_ge(root_done, i + 1)
                V.reciprocal(rinv[0:n, i:i + 1], root[0:n, i:i + 1]).then_inc(rinv_done, 1)
                dve.wait_ge(rinv_done, i + 1)
                V.scalar_tensor_tensor(out=x_slot(i)[0:n, :], in0=x_slot(i)[0:n, :], scalar=rinv[0:n, i:i + 1],
                                       in1=gin[0:n, :], op0=ALU.mult, op1=ALU.mult).then_inc(xn_ready, 1)
                if i >= 2:
                    z_low(i - 2)
            z_low(XT - 2)
            z_low(XT - 1)
            dve.wait_ge(cst_ready, 1)

            def taps(j, k0, k1):
                for k in range(k0, k1):
                    for h in range(2):
                        dst = at(c, j)[:, h * HALF:(h + 1) * HALF] if isinstance(j, int) else \
                            c[:, bass.ds(j, 1), h * HALF:(h + 1) * HALF].rearrange("p a n -> p (a n)")
                        src = ua[:, h * HALF + k:h * HALF + k + HALF]
                        if k == 0:
                            V.tensor_scalar(dst, src, const(j, 0), const(j, C_BIAS), ALU.mult, ALU.add)\
                                .then_inc(conv_step, 1)
                        else:
                            dve.wait_ge(conv_step, j * CONV_OPS + (2 * k + h - 1))
                            V.scalar_tensor_tensor(out=dst, in0=src, scalar=const(j, k), in1=dst,
                                                   op0=ALU.mult, op1=ALU.add).then_inc(conv_step, 1)

            SPLIT = [0, 7, 14, 18, 24, 28, TAPS_A]

            def sample_a(j):
                dst = c[:, j, SEQ:TOK] if isinstance(j, int) else \
                    c[:, bass.ds(j, 1), SEQ:TOK].rearrange("p a n -> p (a n)")
                dve.wait_ge(sa_in, 2 * j + 2)
                w = const(j, 0, TAPS_A).unsqueeze(1).broadcast_to([P, DEC, TAPS_A])
                V.tensor_tensor(sa[:, :, :], sa[:, :, :], w, ALU.mult).then_inc(samp_step, 1)
                dve.wait_ge(samp_step, 3 * j + 1)
                V.tensor_reduce(dst, sa[:, :, :], mybir.AxisListType.X, ALU.add).then_inc(samp_step, 1)
                dve.wait_ge(samp_step, 3 * j + 2)
                V.tensor_scalar(dst, dst, const(j, C_BIAS), None, ALU.add).then_inc(samp_step, 1)

            def finish_b(j):
                dve.wait_ge(bsig_ready, j + 1)
                dve.wait_ge(yb_step, 3 * j + 1)
                V.tensor_tensor(chunked(t1[:, 0:TOK], CW), item_psum(1, CW), chunked(t1[:, 0:TOK], CW), ALU.mult)\
                    .then_inc(yb_step, 1)
                dve.wait_ge(yb_step, 3 * j + 2)
                V.tensor_tensor(t1[:, 0:TOK], t1[:, 0:TOK], t2[:, 0:TOK], ALU.mult).then_inc(yb_step, 1)
                taps(j, SPLIT[4], SPLIT[5])
                dve.wait_ge(yhi_ready, j + 1)
                V.tensor_tensor(at(y_lo, j), t1[:, 0:TOK], f(at(y_hi, j)), ALU.subtract).then_inc(ylo_ready, 1)
                taps(j, SPLIT[5], SPLIT[6])

            def phase1_dve(j):
                n0 = j * len(PH1)
                first = isinstance(j, int) and j == 0
                if not first:
                    finish_b(j - 1)
                dve.wait_ge(chunk_done, item_end(n0 + 1))
                dve.wait_ge(glu_ready, j + 1)
                wait(dve, conv_step, j * CONV_OPS)
                wait(dve, tail_ready, 2 * j)
                V.tensor_tensor(chunked(ua[:, LEAD:LEAD + ZT], CWM), item_psum(1, CWM), chunked(t1[:, :], CWM),
                                ALU.mult).then_inc(ua_ready, 1)
                dve.wait_ge(ua_ready, j + 1)
                taps(j, SPLIT[0], SPLIT[1])
                sample_a(j)
                taps(j, SPLIT[1], SPLIT[2])
                dve.wait_ge(chunk_done, item_end(n0 + 3))
                dve.wait_ge(bh_ready, j + 1)
                ub = chunked(t2[:, 0:CHUNKS * CWB], CWB)
                V.tensor_tensor(ub, item_psum(1, CWB), ub, ALU.mult).then_inc(ub_ready, 1)
                dve.wait_ge(ub_ready, j + 1)
                lead = META - BUF_B - SKIP
                V.tensor_scalar(t1[:, 0:SEQ], t2[:, lead:lead + SEQ], const(j, C_TB), None, ALU.mult)\
                    .then_inc(cb_step, 1)
                for k in range(1, TAPS_B):
                    dve.wait_ge(cb_step, 5 * j + k)
                    V.scalar_tensor_tensor(out=t1[:, 0:SEQ], in0=t2[:, lead + k:lead + k + SEQ],
                                           scalar=const(j, C_TB + k), in1=t1[:, 0:SEQ],
                                           op0=ALU.mult, op1=ALU.add).then_inc(cb_step, 1)
                taps(j, SPLIT[2], SPLIT[3])
                dve.wait_ge(sb_in, 2 * j + 2)
                w = const(j, C_TB, TAPS_B).unsqueeze(1).broadcast_to([P, DEC, TAPS_B])
                V.tensor_tensor(sbw[:, :, :], sbw[:, :, :], w, ALU.mult).then_inc(cb_step, 1)
                dve.wait_ge(cb_step, 5 * j + 4)
                V.tensor_reduce(t1[:, SEQ:TOK], sbw[:, :, :], mybir.AxisListType.X, ALU.add).then_inc(cb_step, 1)
                dve.wait_ge(cb_step, 5 * j + 5)
                dve.wait_ge(chunk_done, item_end(n0 + 4))
                V.tensor_tensor(chunked(t1[:, 0:TOK], CW), item_psum(0, CW), chunked(t1[:, 0:TOK], CW), ALU.mult)\
                    .then_inc(yb_step, 1)
                taps(j, SPLIT[3], SPLIT[4])

            phase1_dve(0)
            with dve.Fori(1, K) as j:
                phase1_dve(j)
            finish_b(K - 1)

            def merge_b(j):
                dve.wait_ge(chunk_done, item_end(I2 + 2 * j + 1))
                dve.wait_ge(mb_ready, j + 1)
                if isinstance(j, int) and j == 0:
                    dve.wait_ge(yb_step, 3 * K)
                else:
                    dve.wait_ge(spilled, 16 * j)
                V.tensor_tensor(chunked(t2[:, 0:TOK], CW), item_psum(1, CW), chunked(t1[:, 0:TOK], CW), ALU.mult)\
                    .then_inc(mbp_ready, 1)

            row = ua[:, 0:TOK]
            dve.wait_ge(conv_step, K * CONV_OPS)
            dve.wait_ge(samp_step, 3 * K)
            dve.wait_ge(tail_ready, 2 * K)
            V.tensor_tensor(row, c[:, 0, :], c[:, 1, :], ALU.add).then_inc(sum_step, 1)
            for j in range(2, K):
                dve.wait_ge(sum_step, j - 1)
                V.tensor_tensor(row, row, c[:, j, :], ALU.add).then_inc(sum_step, 1)
            merge_b(0)
            merge_b(1)
            dve.wait_ge(mean_ready, CHUNKS)
            for j in range(K):
                V.tensor_tensor(c[:, j, :], c[:, j, :], row, ALU.subtract).then_inc(sub_done, 1)
            dve.wait_ge(sub_done, K)
            for j in range(K):
                dve.wait_ge(sqr_ready, j + 1)
                if j == 0:
                    V.tensor_copy(row, sq[:, :]).then_inc(sqacc_step, 1)
                else:
                    dve.wait_ge(sqacc_step, j)
                    V.tensor_tensor(row, row, sq[:, :], ALU.add).then_inc(sqacc_step, 1)
                if j == 4:
                    merge_b(2)
            merge_b(3)
            dve.wait_ge(std_ready, CHUNKS)
            V.reciprocal(row, row).then_inc(rstd_ready, 1)
            dve.wait_ge(rstd_ready, 1)
            for j in range(K):
                V.tensor_tensor(c[:, j, :], c[:, j, :], row, ALU.mult).then_inc(ln_done, 1)
            with dve.Fori(4, K) as j:
                merge_b(j)

            def phase3_dve(j):
                dve.wait_ge(nsig_ready, j + 1)
                V.tensor_scalar(at(c, j), at(c, j), const(j, C_LNG), const(j, C_LNB), ALU.mult, ALU.add)\
                    .then_inc(ya_step, 1)
                dve.wait_ge(ya_step, 4 * j + 1)
                V.tensor_tensor(t2[:, 0:TOK], t2[:, 0:TOK], at(c, j), ALU.mult).then_inc(ya_step, 1)
                dve.wait_ge(ya_step, 4 * j + 2)
                dve.wait_ge(asig_ready, j + 1)
                V.tensor_tensor(chunked(t2[:, 0:TOK], CW), item_psum(0, CW), chunked(t2[:, 0:TOK], CW), ALU.mult)\
                    .then_inc(ya_step, 1)
                dve.wait_ge(ya_step, 4 * j + 3)
                V.tensor_tensor(t2[:, 0:TOK], t2[:, 0:TOK], t1[:, 0:TOK], ALU.mult).then_inc(ya_step, 1)
                dve.wait_ge(ahi_ready, j + 1)
                V.tensor_tensor(at(y_lo, j), t2[:, 0:TOK], f(at(y_hi, j)), ALU.subtract).then_inc(alo_ready, 1)

            dve.wait_ge(ln_done, K)
            with dve.Fori(0, K) as j:
                phase3_dve(j)

            dve.wait_ge(ma_ready, K)

            def merge_a(j, s):
                dve.wait_ge(mb_back[s], (j - s) * 8 + 16)
                for ch in range(CHUNKS):
                    dst = c[:, j, CW * ch:CW * (ch + 1)] if isinstance(j, int) else \
                        c[:, bass.ds(j, 1), CW * ch:CW * (ch + 1)].rearrange("p a n -> p (a n)")
                    dve.wait_ge(chunk_done, (j + I4) * CHUNKS + (ch + 1))
                    V.tensor_tensor(dst, ps[s][:, ch, 0:CW], dst, ALU.mult).then_inc(mul_done, 1)
                    dve.wait_ge(mul_done, j * CHUNKS + (ch + 1))
                    V.tensor_tensor(dst, dst, (t1, t2)[s][:, CW * ch:CW * (ch + 1)], ALU.add).then_inc(merged_done, 1)

            with dve.Fori(0, K // 2) as jj:
                for s in range(2):
                    merge_a(2 * jj + s, s)

            dve.wait_ge(gf_in, 16)

            def residual(i, s, n=P):
                t = (t1, t2)[s]
                dve.wait_ge(out_mm, i + 1)
                dve.wait_ge(xr_in[s], (i - s) * 8 + 16)
                tv = t[0:n, 0:D].rearrange("p (h e) -> p h e", h=2)
                V.tensor_tensor(tv, ps[s][0:n, 0:2, :], tv, ALU.add).then_inc(h_ready, 1)

            def scale_rows(i, s, n=P):
                t = (t1, t2)[s]
                a = root[0:n, XT + i:XT + i + 1] if isinstance(i, int) else root[0:n, bass.ds(i + XT, 1)]
                b = rinv[0:n, XT + i:XT + i + 1] if isinstance(i, int) else rinv[0:n, bass.ds(i + XT, 1)]
                dve.wait_ge(hroot_done, i + 1)
                V.reciprocal(b, a).then_inc(hinv_done, 1)
                dve.wait_ge(hinv_done, i + 1)
                V.scalar_tensor_tensor(out=t[0:n, 0:D], in0=t[0:n, 0:D], scalar=b, in1=gfin[0:n, :],
                                       op0=ALU.mult, op1=ALU.mult).then_inc(y_ready, 1)

            with dve.Fori(0, (TT - 1) // 2) as ii:
                for s in range(2):
                    residual(2 * ii + s, s)
                    scale_rows(2 * ii + s, s)
            residual(TT - 1, 0, LAST5)
            scale_rows(TT - 1, 0, LAST5)

        @block.tensor
        def _(pe):
            def chunk(s, hi, lo, off, width, ch, k0=0, k1=K):
                lo_col, hi_col = off + ch * width, off + (ch + 1) * width
                for k in range(k0, k1):
                    parts = ((w_hi, hi), (w_hi, lo), (w_lo, hi))
                    for n, (w, x) in enumerate(parts):
                        last = nc.tensor.matmul(ps[s][:, ch, 0:width], w[:, s, k, :], x[:, k, lo_col:hi_col],
                                                start=(k == 0 and n == 0), stop=(k == K - 1 and n == 2))
                if k1 == K:
                    last.then_inc(chunk_done, 1)

            def item(s, hi, lo, off, width):
                for ch in range(CHUNKS):
                    chunk(s, hi, lo, off, width, ch)

            def transpose_x(i):
                n = x_rows(i)
                pe.wait_ge(xn_ready, i + 1)
                for h in range(2):
                    wait(pe, zlo_done, 2 * i + h - 3)
                    for k in range(4):
                        col = (4 * h + k) * P
                        last = nc.tensor.transpose(x_bank(i, h)[:, k * P:k * P + n], x_slot(i)[0:n, col:col + P],
                                                   ident[0:n, 0:n])
                    last.then_inc(xt_done, 1)

            pe.wait_ge(pool_const, 3)
            for i in range(3):
                transpose_x(i)
            pe.wait_ge(zlo_done, 6)
            pe.wait_ge(lo_ready, 1)
            def first_chunk(s, ch, between):
                chunk(s, z_hi, z_lo, 0, CWM, ch, 0, K // 2)
                if between:
                    transpose_x(between[0])
                chunk(s, z_hi, z_lo, 0, CWM, ch, K // 2, K)
                if between[1:]:
                    transpose_x(between[1])

            first_chunk(0, 0, [3, 4])
            pe.wait_ge(lo_ready, 2)
            first_chunk(1, 0, [5, 6])
            pe.wait_ge(zlo_done, 12)
            first_chunk(0, 1, [7, 8])
            pe.wait_ge(zlo_done, 16)
            first_chunk(1, 1, [])
            pe.wait_ge(zlo_done, 2 * XT)
            pe.wait_ge(pool_const, 7)
            pe.wait_ge(cst_in, 80)
            for k in range(K):
                last = nc.tensor.transpose(spare[0][:, k * CONSTS:(k + 1) * CONSTS], sq[0:CONSTS, k * P:(k + 1) * P],
                                           ident[0:CONSTS, 0:CONSTS])
            last.then_inc(cst_t, 1)
            chunk(0, z_hi, z_lo, 0, CWM, 2)
            chunk(1, z_hi, z_lo, 0, CWM, 2)

            def transpose_tails(j):
                pe.wait_ge(tail_ready, 2 * j + 2)
                wait(pe, tail_rows, j)
                nc.tensor.transpose(spare[1][:, 0:P], tail_in[:, :], ident[:, :]).then_inc(tail_t, 1)

            def transpose_states(j):
                pe.wait_ge(st_in, 32 * j + 32)
                if isinstance(j, int) and j == 0:
                    pe.wait_ge(cst_ready, 1)
                else:
                    pe.wait_ge(sb_in, 2 * j - 1)
                for h in range(2):
                    nc.tensor.transpose(spare[0][:, h * P:(h + 1) * P], st_raw[:, h, :], ident[:, :]).then_inc(st_t, 1)

            def phase1_pe(j):
                n0 = j * len(PH1)
                first = isinstance(j, int) and j == 0
                freed = [(yb_step, 3 * j - 2), (yb_step, 3 * j - 1), (glu_ready, j + 1), (ua_ready, j + 1),
                         (bh_ready, j + 1), (ub_ready, j + 1)]
                for s, (_, off, width) in enumerate(PH1):
                    if s == (2 if first else 0):
                        transpose_states(j)
                    if s == 1 and not first:
                        transpose_tails(j - 1)
                    if first and s < 2:
                        continue
                    pe.wait_ge(lo_ready, n0 + s + 1)
                    pe.wait_ge(*freed[s])
                    item(s % 2, z_hi, z_lo, off, width)

            phase1_pe(0)
            with pe.Fori(1, K) as j:
                phase1_pe(j)

            def phase2_pe(j):
                n0 = I2 + 2 * j
                first = isinstance(j, int) and j == 0
                pe.wait_ge(lo_ready, n0 + 1)
                pe.wait_ge(*((yb_step, 3 * K - 2) if first else (mb_ready, j)))
                item(0, z_hi, z_lo, META, CW)
                if first:
                    transpose_tails(K - 1)
                    pe.wait_ge(ylo_ready, K)
                pe.wait_ge(lo_ready, n0 + 2)
                pe.wait_ge(*((yb_step, 3 * K - 1) if first else (mbp_ready, j)))
                item(1, y_hi, y_lo, 0, CW)

            def column_means(ready, value, left, done):
                pe.wait_ge(ready, value)
                for ch in range(CHUNKS):
                    if ch == 2:
                        pe.wait_ge(left, 1)
                    nc.tensor.matmul(spare[ch % 2][:, 0:CW], ident[:, :], ua[:, CW * ch:CW * (ch + 1)],
                                     start=True, stop=True).then_inc(done, 1)

            phase2_pe(0)
            phase2_pe(1)
            pe.wait_ge(pool_const, 8)
            pe.wait_ge(tail_rows, K)
            column_means(sum_step, K - 1, mean_ready, mean_t)
            phase2_pe(2)
            phase2_pe(3)
            column_means(sqacc_step, K, std_ready, var_t)
            with pe.Fori(4, K) as j:
                phase2_pe(j)

            def phase3_pe(j):
                n0 = I3 + 2 * j
                first = isinstance(j, int) and j == 0
                pe.wait_ge(lo_ready, n0 + 1)
                pe.wait_ge(*((mb_ready, K) if first else (ya_step, 4 * j - 1)))
                item(0, z_hi, z_lo, META, CW)
                pe.wait_ge(lo_ready, n0 + 2)
                pe.wait_ge(*((mbp_ready, K) if first else (ma_ready, j)))
                item(1, z_hi, z_lo, META, CW)

            phase3_pe(0)
            with pe.Fori(1, K) as j:
                phase3_pe(j)

            pe.wait_ge(alo_ready, K)

            def phase4_pe(j, s, split):
                pe.wait_ge(lo_ready, split + 1)
                if isinstance(j, int) and j < 2:
                    pe.wait_ge(*((ya_step, 4 * K - 1), (ma_ready, K))[j])
                else:
                    pe.wait_ge(mul_done, j * CHUNKS - CHUNKS)
                item(s, y_hi, y_lo, 0, CW)

            phase4_pe(0, 0, I4)
            phase4_pe(1, 1, I4 + 1)
            with pe.Fori(1, K // 2) as jj:
                for s in range(2):
                    phase4_pe(2 * jj + s, s, I4 + 4 * jj + 2 * s - 1)

            def out_tile(i, s, n=P):
                pe.wait_ge(lo_ready, i + (I4 + 2 * K + 1))
                if isinstance(i, int) and i < 2:
                    pe.wait_ge(mul_done, CHUNKS * (K - 1 + i))
                else:
                    pe.wait_ge(h_ready, i - 1)
                for h in range(2):
                    for k in range(K):
                        parts = ((w_hi, w_out_hi), (w_hi, w_out_lo), (w_lo, w_out_hi))
                        for m, (x, w) in enumerate(parts):
                            last = nc.tensor.matmul(ps[s][0:n, h, :], x[:, s, k, 0:n], w[:, k, h * 512:(h + 1) * 512],
                                                    start=(k == 0 and m == 0), stop=(k == K - 1 and m == 2))
                last.then_inc(out_mm, 1)

            out_tile(0, 0)
            out_tile(1, 1)
            with pe.Fori(1, (TT - 1) // 2) as ii:
                for s in range(2):
                    out_tile(2 * ii + s, s)
            out_tile(TT - 1, 0, LAST5)


_INS = ["x_prompt", "x_sample", "state_conv_a", "state_conv_b", "meta_tokens", "norm_g", "w_in", "conv_a_w",
        "conv_a_b", "ln_a_g", "ln_a_b", "conv_b_w", "w_pa", "w_pb", "w_out", "final_norm_g"]
_OUTS = [(1, 1024, 1024), (8, 1, 1024), (1, 1, 30, 1024), (1, 1, 2, 1024), (1, 8, 30, 1024), (1, 8, 2, 1024)]


def kernel(**inputs):
    import numpy as _np
    import concourse.bacc as _bacc
    from concourse import mybir as _mybir
    from concourse.bass_utils import run_bass_kernel_spmd as _run

    nc = _bacc.Bacc("TRN2", target_bir_lowering=False, num_devices=1)
    arrays, args = {}, []
    for name in _INS:
        a = _np.ascontiguousarray(inputs[name])
        arrays[f"in_{name}_dram"] = a
        args.append(nc.dram_tensor(f"in_{name}_dram", a.shape, _mybir.dt.from_np(a.dtype), kind="ExternalInput").ap())
    for i, shape in enumerate(_OUTS):
        args.append(nc.dram_tensor(f"out_{i}_dram", shape, _mybir.dt.float32, kind="ExternalOutput").ap())
    decoder_step(nc, *args)
    r = _run(nc, [arrays], core_ids=[0])
    return tuple(r.results[0][f"out_{i}_dram"] for i in range(len(_OUTS)))
```

```python
from contextlib import ExitStack

import concourse.bass as bass
from concourse import mybir
from concourse.alu_op_type import AluOpType as ALU

ACT = mybir.ActivationFunctionType
F32 = mybir.dt.float32
F32R = mybir.dt.float32r

P = 128
QUAD = 32
RMS_EPS, LN_EPS = 1e-6, 1e-5


def wait(eng, sem, value):
    if not isinstance(value, int) or value > 0:
        eng.wait_ge(sem, value)


def decoder_step(nc, x_prompt, x_sample, state_conv_a, state_conv_b, meta_tokens, norm_g, w_in, conv_a_w,
                 conv_a_b, ln_a_g, ln_a_b, conv_b_w, w_pa, w_pb, w_out, final_norm_g,
                 y_prompt, y_sample, new_a_prompt, new_b_prompt, new_a_sample, new_b_sample):
    _, SEQ, D = x_prompt.shape
    DEC = x_sample.shape[0]
    META = meta_tokens.shape[0]
    TAPS_A, TAPS_B = conv_a_w.shape[1], conv_b_w.shape[1]
    BUF_A, BUF_B = TAPS_A - 1, TAPS_B - 1
    K = D // P
    TOK = SEQ + DEC
    ALL = META + TOK
    CHUNKS = 3
    CW = TOK // CHUNKS
    CWM = CW + 6
    ZT = CHUNKS * CWM
    CWB = CW + 2
    SKIP = ZT - CHUNKS * CWB
    assert D == 1024 and SEQ == 1024 and DEC == 8 and META == 16 and CW * CHUNKS == TOK and ZT >= ALL and SKIP <= META - BUF_B
    HALF, PAIRS = SEQ // 2, BUF_A // 2
    assert BUF_A % 2 == 0 and SEQ % 4 == 0
    LEAD = BUF_A - META
    UA_S = BUF_A + SEQ
    UB_S = META + SEQ - SKIP
    TAIL_A, TAIL_B = BUF_A + DEC, BUF_B + DEC
    TAIL = TAIL_A + TAIL_B
    A_VAL, A_GLU, A_GATE, B_H, B_C, B_B, B_GATE, M_A, M_B = (D * i for i in range(9))
    PH1 = [(A_GLU, 0, CWM), (A_VAL, 0, CWM), (B_H, SKIP, CWB), (B_C, SKIP, CWB), (B_B, META, CW), (B_GATE, META, CW)]
    N1, N2, N3, N4 = len(PH1) * K, 2 * K, 2 * K, K
    I2, I3, I4, I5 = N1, N1 + N2, N1 + N2 + N3, N1 + N2 + N3 + N4
    TT = (TOK + P - 1) // P
    XT = (ALL + P - 1) // P
    LASTX = ALL - P * (XT - 1)
    OP_AB, OP_S = 1, 1 + 2 * PAIRS
    OP_C, OP_END = OP_S + 1, OP_S + 1 + 2 * PAIRS
    CONV_OPS = OP_END + 5
    CONSTS = TAPS_A + TAPS_B + 3
    C_TB, C_BIAS, C_LNG, C_LNB = TAPS_A, TAPS_A + TAPS_B, TAPS_A + TAPS_B + 1, TAPS_A + TAPS_B + 2

    spill = nc.dram_tensor("merged_b_spill", [P, K, TOK], F32).ap()

    with ExitStack() as ctx:
        def sb(name, shape, dt=F32):
            return ctx.enter_context(nc.sbuf_tensor(name, shape, dt))

        def pb(name, shape):
            return ctx.enter_context(nc.psum_tensor(name, shape, F32))

        def sem(name):
            return ctx.enter_context(nc.semaphore(name))

        z_hi = sb("z_hi", [P, K, ZT], F32R)
        z_lo = sb("z_lo", [P, K, ZT], F32R)
        y_hi = sb("y_hi", [P, K, TOK], F32R)
        y_lo = sb("y_lo", [P, K, TOK], F32R)
        c = sb("c", [P, K, TOK])
        w_hi = sb("w_hi", [P, 2, K, P], F32R)
        w_lo = sb("w_lo", [P, 2, K, P], F32R)
        raw = sb("raw", [P, 2, K, P])
        t1 = sb("t1", [P, ZT])
        t2 = sb("t2", [P, CHUNKS * CWB])
        ua = sb("ua", [P, LEAD + ZT])
        sq = sb("sq", [P, TOK])
        st_raw = sb("st_raw", [P, 2, P])
        sa = sb("sa", [P, DEC, TAPS_A])
        sbw = sb("sbw", [P, DEC, TAPS_B])
        tail_in = sb("tail_in", [P, TAIL])
        tail_out = sb("tail_out", [TAIL, P])
        cst = sb("cst", [P, K, CONSTS])
        tap_sum = sb("tap_sum", [P, K, PAIRS])
        ident = sb("ident", [P, P])
        ssum = sb("ssum", [P, XT])
        root = sb("root", [P, XT])
        rinv = sb("rinv", [P, XT])
        eps = sb("eps", [P, 2])
        gfin = ua[:, 0:D]

        w_out_hi = z_hi[:, :, :].rearrange("p k t -> p (k t)")[:, 0:K * D].rearrange("p (k e) -> p k e", k=K)
        w_out_lo = z_lo[:, :, :].rearrange("p k t -> p (k t)")[:, 0:K * D].rearrange("p (k e) -> p k e", k=K)

        ps = [pb("ps0", [P, CHUNKS, 512]), pb("ps1", [P, CHUNKS, 512])]
        spare = [pb("spare0", [P, 512]), pb("spare1", [P, 512])]

        x_in = [sem(f"x_in{i}") for i in range(XT)]
        gin_in, cst_in, raw_in = sem("gin_in"), sem("cst_in"), [sem("raw_in0"), sem("raw_in1")]
        pool_const = sem("pool_const")
        sq_done, root_done, xn_ready, rinv_done = sem("sq_done"), sem("root_done"), sem("xn_ready"), sem("rinv_done")
        xt_done, zhi_done, zlo_done = sem("xt_done"), sem("zhi_done"), sem("zlo_done")
        cst_t, cst_ready = sem("cst_t"), sem("cst_ready")
        hi_ready, lo_ready = sem("hi_ready"), sem("lo_ready")
        chunk_done = sem("chunk_done")
        glu_ready, ua_ready, bh_ready, ub_ready, bsig_ready = (
            sem("glu_ready"), sem("ua_ready"), sem("bh_ready"), sem("ub_ready"), sem("bsig_ready"))
        taps_ready, conv_step, cb_step, samp_step, yb_step = sem("taps_ready"), sem("conv_step"), sem("cb_step"), sem("samp_step"), sem("yb_step")
        yhi_ready, ylo_ready = sem("yhi_ready"), sem("ylo_ready")
        st_in, st_t, sa_in, sb_in = sem("st_in"), sem("st_t"), sem("sa_in"), sem("sb_in")
        tail_ready, tail_t, tail_rows, state_stored = sem("tail_ready"), sem("tail_t"), sem("tail_rows"), sem("state_stored")
        mb_ready, mbp_ready, spilled = sem("mb_ready"), sem("mbp_ready"), sem("spilled")
        sum_step, mean_t, mean_ready, sub_done = sem("sum_step"), sem("mean_t"), sem("mean_ready"), sem("sub_done")
        sqr_ready, sqacc_step, var_t, std_ready, rstd_ready, ln_done = (
            sem("sqr_ready"), sem("sqacc_step"), sem("var_t"), sem("std_ready"), sem("rstd_ready"), sem("ln_done"))
        asig_ready, nsig_ready, ya_step, ahi_ready, alo_ready, ma_ready = (
            sem("asig_ready"), sem("nsig_ready"), sem("ya_step"), sem("ahi_ready"), sem("alo_ready"), sem("ma_ready"))
        mb_back, mul_done, merged_done = [sem("mb_back0"), sem("mb_back1")], sem("mul_done"), sem("merged_done")
        out_mm, xr_in, gf_in = sem("out_mm"), [sem("xr_in0"), sem("xr_in1")], sem("gf_in")
        half_added = sem("half_added")
        h_ready, hsq_done, hroot_done, hinv_done, y_ready = (
            sem("h_ready"), sem("hsq_done"), sem("hroot_done"), sem("hinv_done"), sem("y_ready"))
        y_stored = [sem("y_stored0"), sem("y_stored1")]

        def at(tensor, j):
            if isinstance(j, int):
                return tensor[:, j, :]
            return tensor[:, bass.ds(j, 1), :].rearrange("p a n -> p (a n)")

        def const(j, i, n=1):
            if isinstance(j, int):
                return cst[:, j, i:i + n]
            return cst[:, bass.ds(j, 1), i:i + n].rearrange("p a n -> p (a n)")

        def f(ap):
            return ap.bitcast(F32)

        def item_psum(s, width):
            return ps[s][:, :, 0:width]

        def chunked(ap, width):
            return ap.rearrange("p (c w) -> p c w", w=width)

        def item_end(n):
            if isinstance(n, int) and n == 0:
                return 2 * CHUNKS - 1
            return (n + 1) * CHUNKS

        def x_slot(i):
            return c[:, i, 0:D] if i < K - 1 else (t1 if i == K - 1 else t2)[:, 0:D]

        def x_bank(i, h):
            return spare[h][:, :] if i % 2 == 0 else ps[1][:, 1 + h, :]

        gin = c[:, K - 1, 0:D]

        def x_rows(i):
            return P if i < XT - 1 else LASTX

        def w_src(w, col):
            if isinstance(col, int):
                return w[0, :, col:col + P].rearrange("(k p) e -> p k e", p=P)
            return w[0, :, bass.ds(col, P)].rearrange("(k p) e -> p k e", p=P)

        block = ctx.enter_context(nc.Block())

        @block.sync
        def _(sp):
            def load_item(q, s, w, col):
                src = w_src(w, col)
                wait(sp, lo_ready, q - 1)
                sp.dma_start(raw[:, s, :, :], src).then_inc(raw_in[s], 16)

            def load_x(i):
                dst = x_slot(i)
                if i == 0:
                    sp.dma_start(dst[0:META, :], meta_tokens[:, :]).then_inc(x_in[0], 16)
                    sp.dma_start(dst[META:P, :], x_prompt[0, 0:P - META, :]).then_inc(x_in[0], 16)
                elif i < XT - 1:
                    sp.dma_start(dst[:, :], x_prompt[0, P * i - META:P * (i + 1) - META, :]).then_inc(x_in[i], 16)
                else:
                    n = SEQ - (P * i - META)
                    sp.dma_start(dst[0:n, :], x_prompt[0, P * i - META:SEQ, :]).then_inc(x_in[i], 16)
                    sp.dma_start(dst[n:n + DEC, :], x_sample[:, 0, :]).then_inc(x_in[i], 16)

            for i in range(XT):
                load_x(i)
                if i == 0:
                    sp.dma_start(gin, norm_g[0, :].partition_broadcast(P)).then_inc(gin_in, 16)
                if i == 2:
                    load_item(0, 0, w_in, PH1[0][0])
                if i == 3:
                    load_item(1, 1, w_in, PH1[1][0])
            for src, r0, n in ((conv_a_w[0, :, :], 0, TAPS_A), (conv_b_w[0, :, :], C_TB, TAPS_B),
                               (conv_a_b[0:1, :], C_BIAS, 1), (ln_a_g[0:1, :], C_LNG, 1), (ln_a_b[0:1, :], C_LNB, 1)):
                sp.dma_start(sq[r0:r0 + n, 0:D], src).then_inc(cst_in, 16)

            def phase1(j, first=0):
                wait(sp, st_t, 2 * j)
                cols = slice(P * j, P * (j + 1)) if isinstance(j, int) else bass.ds(P * j, P)
                sp.dma_start(st_raw[0:4 * BUF_A, :, :],
                             state_conv_a[0, :, :, cols].rearrange("(h b) r e -> (b r) h e", h=2)).then_inc(st_in, 16)
                sp.dma_start(st_raw[4 * BUF_A:4 * (BUF_A + BUF_B), :, :],
                             state_conv_b[0, :, :, cols].rearrange("(h b) r e -> (b r) h e", h=2)).then_inc(st_in, 16)
                for s, (col, _, _) in enumerate(PH1):
                    if s < first:
                        continue
                    load_item(j * len(PH1) + s, s % 2, w_in, j * P + col)
                    if s == 3 and not (isinstance(j, int) and j == 0):
                        store_tails(j - 1)

            def store_tails(j):
                wait(sp, tail_rows, j + 1)
                cols = slice(P * j, P * (j + 1)) if isinstance(j, int) else bass.ds(P * j, P)
                for dst, r0, n in ((new_a_prompt[0, 0, :, cols], 0, BUF_A),
                                   (new_a_sample[0, :, BUF_A - 1, cols], BUF_A, DEC),
                                   (new_b_prompt[0, 0, :, cols], TAIL_A, BUF_B),
                                   (new_b_sample[0, :, BUF_B - 1, cols], TAIL_A + BUF_B, DEC)):
                    sp.dma_start(dst, tail_out[r0:r0 + n, :]).then_inc(state_stored, 16)

            phase1(0, first=2)
            sp.dma_start(new_a_sample[0, :, 0:BUF_A - 1, :], state_conv_a[0, :, 1:BUF_A, :]).then_inc(state_stored, 16)
            sp.dma_start(new_b_sample[0, :, 0:BUF_B - 1, :], state_conv_b[0, :, 1:BUF_B, :]).then_inc(state_stored, 16)
            with sp.Fori(1, K) as j:
                phase1(j)

            def phase2(j):
                load_item(I2 + 2 * j, 0, w_in, j * P + M_B)
                load_item(I2 + 2 * j + 1, 1, w_pb, (j + 1) * P - P)
                if not (isinstance(j, int) and j == 0):
                    spill_out(j - 1)

            def spill_out(j):
                wait(sp, mbp_ready, j + 1)
                dst = spill[:, j, :] if isinstance(j, int) else spill[:, bass.ds(j, 1), :].rearrange("p a n -> p (a n)")
                sp.dma_start(dst, t2[:, 0:TOK]).then_inc(spilled, 16)

            phase2(0)
            phase2(1)
            store_tails(K - 1)
            with sp.Fori(2, K) as j:
                phase2(j)

            def phase3(j):
                load_item(I3 + 2 * j, 0, w_in, j * P + A_GATE)
                load_item(I3 + 2 * j + 1, 1, w_in, j * P + M_A)

            phase3(0)
            spill_out(K - 1)
            with sp.Fori(1, K) as j:
                phase3(j)

            def load_back(j, s):
                t = (t1, t2)[s]
                if isinstance(j, int) and j < 2:
                    wait(sp, alo_ready, K)
                    wait(sp, spilled, 16 * K)
                else:
                    wait(sp, merged_done, CHUNKS * (j - 1))
                src = spill[:, j, :] if isinstance(j, int) else spill[:, bass.ds(j, 1), :].rearrange("p a n -> p (a n)")
                sp.dma_start(t[:, 0:TOK], src).then_inc(mb_back[s], 16)

            def load_out_rows(q, s, m):
                wait(sp, lo_ready, q - 1)
                rows = slice(P * m, P * (m + 1)) if isinstance(m, int) else bass.ds(P * m, P)
                sp.dma_start(raw[:, s, :, :].rearrange("p k e -> p (k e)"), w_out[0, rows, :]).then_inc(raw_in[s], 16)

            load_item(I4, 0, w_pa, 0)
            load_item(I4 + 1, 1, w_pa, P)
            load_back(0, 0)
            load_back(1, 1)

            def phase4(m, s):
                load_out_rows(I4 + 2 + 2 * m, 0, m)
                load_item(I4 + 3 + 2 * m, 1, w_pa, m * P + 2 * P)
                load_back(m + 2, s)

            phase4(0, 0)
            phase4(1, 1)
            with sp.Fori(1, (K - 2) // 2) as jj:
                phase4(2 * jj, 0)
                phase4(2 * jj + 1, 1)
            load_out_rows(I4 + 2 * K - 2, 0, K - 2)
            load_out_rows(I4 + 2 * K - 1, 1, K - 1)

            wait(sp, ln_done, K)
            sp.dma_start(gfin, final_norm_g.partition_broadcast(P)).then_inc(gf_in, 16)

            def load_res(i, s):
                if isinstance(i, int) and i < 2:
                    wait(sp, merged_done, CHUNKS * (K - 1 + i))
                else:
                    wait(sp, y_stored[s], 8 * (i - s))
                t = (t1, t2)[s]
                if isinstance(i, int) and i == TT - 1:
                    sp.dma_start(t[0:DEC, 0:D], x_sample[:, 0, :]).then_inc(xr_in[s], 16)
                else:
                    rows = slice(P * i, P * (i + 1)) if isinstance(i, int) else bass.ds(P * i, P)
                    sp.dma_start(t[:, 0:D], x_prompt[0, rows, :]).then_inc(xr_in[s], 16)

            def store_y(i, s):
                wait(sp, y_ready, i + 1)
                t = (t1, t2)[s]
                if isinstance(i, int) and i == TT - 1:
                    sp.dma_start(y_sample[:, 0, :], t[0:DEC, 0:D]).then_inc(y_stored[s], 16)
                else:
                    rows = slice(P * i, P * (i + 1)) if isinstance(i, int) else bass.ds(P * i, P)
                    sp.dma_start(y_prompt[0, rows, :], t[:, 0:D]).then_inc(y_stored[s], 16)

            load_res(0, 0)
            load_res(1, 1)
            with sp.Fori(0, (TT - 1) // 2 - 1) as ii:
                for s in range(2):
                    store_y(2 * ii + s, s)
                    load_res(2 * ii + s + 2, s)
            store_y(TT - 3, 0)
            load_res(TT - 1, 0)
            store_y(TT - 2, 1)
            store_y(TT - 1, 0)
            sp.wait_ge(y_stored[0], 16 * ((TT + 1) // 2))
            sp.wait_ge(y_stored[1], 16 * (TT // 2))
            sp.wait_ge(state_stored, 32 + 64 * K)
            sp.wait_ge(spilled, 16 * K)

        @block.gpsimd
        def _(pool):
            nc.gpsimd.memset(eps[:, 0:1], RMS_EPS)
            nc.gpsimd.memset(eps[:, 1:2], LN_EPS).then_inc(pool_const, 1)
            nc.gpsimd.memset(ident[:, :], 0.0).then_inc(pool_const, 1)
            pool.wait_ge(pool_const, 2)
            nc.gpsimd.affine_select(out=ident[:, :], in_=ident[:, :], compare_op=ALU.not_equal, fill=1.0, base=0,
                                    pattern=[[-1, P]], channel_multiplier=1).then_inc(pool_const, 1)
            nc.gpsimd.memset(z_hi[:, :, ALL:ZT].bitcast(F32), 0.0).then_inc(pool_const, 1)
            nc.gpsimd.memset(z_lo[:, :, ALL:ZT].bitcast(F32), 0.0).then_inc(pool_const, 1)
            nc.gpsimd.memset(ua[:, 0:LEAD], 0.0).then_inc(pool_const, 1)

            def lo_weights(q, s):
                pool.wait_ge(hi_ready, q + 1)
                nc.gpsimd.tensor_tensor(w_lo[:, s, :, :], raw[:, s, :, :], f(w_hi[:, s, :, :]), ALU.subtract)\
                    .then_inc(lo_ready, 1)

            lo_weights(0, 0)
            lo_weights(1, 1)
            pool.wait_ge(lo_ready, I2 + 1)
            lo_weights(I2 + 1, 1)
            pool.wait_ge(tail_t, K)
            nc.gpsimd.memset(ident[:, :], 1.0 / D).then_inc(pool_const, 1)
            with pool.Fori(I2 // 2 + 1, I4 // 2 + 1) as qq:
                for s in range(2):
                    lo_weights(2 * qq + s, s)

            def lo_out_rows(q, s, m):
                pool.wait_ge(hi_ready, q + 1)
                nc.gpsimd.tensor_tensor(at(w_out_lo, m), raw[:, s, :, :].rearrange("p k e -> p (k e)"),
                                        f(at(w_out_hi, m)), ALU.subtract).then_inc(lo_ready, 1)

            def lo_pa(q, ring):
                pool.wait_ge(hi_ready, q + 1)
                nc.gpsimd.tensor_tensor(w_lo[:, ring, :, :], raw[:, 1, :, :], f(w_hi[:, ring, :, :]), ALU.subtract)\
                    .then_inc(lo_ready, 1)

            with pool.Fori(0, (K - 2) // 2) as jj:
                for r in range(2):
                    lo_out_rows(I4 + 2 + 2 * r + 4 * jj, 0, 2 * jj + r)
                    lo_pa(I4 + 3 + 2 * r + 4 * jj, r)
            lo_out_rows(I4 + 2 * K - 2, 0, K - 2)
            lo_out_rows(I4 + 2 * K - 1, 1, K - 1)

            Q5 = I4 + 2 * K

            def lo_merged(i, s, n=P):
                pool.wait_ge(hi_ready, Q5 + 1 + i)
                cols = slice(P * i, P * i + n) if isinstance(i, int) else bass.ds(P * i, n)
                nc.gpsimd.tensor_tensor(w_lo[:, s, :, 0:n], c[:, :, cols], f(w_hi[:, s, :, 0:n]), ALU.subtract)\
                    .then_inc(lo_ready, 1)

            with pool.Fori(0, (TT - 1) // 2) as ii:
                for s in range(2):
                    lo_merged(2 * ii + s, s)
            pool.wait_ge(hi_ready, Q5 + TT)
            nc.gpsimd.tensor_tensor(w_hi[:, 0, :, QUAD:QUAD + DEC], c[:, :, SEQ:TOK], f(w_hi[:, 0, :, 0:DEC]),
                                    ALU.subtract).then_inc(lo_ready, 1)

        @block.scalar
        def _(act):

            def hi_weights(q, s, item=None):
                act.wait_ge(raw_in[s], (q - s) * 8 + 16)
                item = q if item is None else item
                if not isinstance(item, int) or item >= 2:
                    act.wait_ge(chunk_done, item_end(item - 2))
                nc.scalar.activation(w_hi[:, s, :, :], raw[:, s, :, :], ACT.Copy).then_inc(hi_ready, 1)

            def z_evacuate(i):
                n = x_rows(i)
                for h in range(2):
                    u = 2 * i + h
                    act.wait_ge(xt_done, u + 1)
                    src = x_bank(i, h).rearrange("p (k t) -> p k t", k=4)[:, :, 0:n]
                    nc.scalar.activation(z_hi[:, 4 * h:4 * h + 4, P * i:P * i + n], src, ACT.Copy).then_inc(zhi_done, 1)

            act.wait_ge(pool_const, 1)
            nc.scalar.activation(root[:, 0:1], eps[:, 0:1], ACT.Sqrt).then_inc(root_done, 1)
            act.wait_ge(root_done, 1)

            def root_mean_square(i):
                n = x_rows(i)
                act.wait_ge(x_in[i], 32 if i in (0, XT - 1) else 16)
                wait(act, sq_done, i)
                nc.scalar.activation(ua[0:n, LEAD + ZT - D:LEAD + ZT], x_slot(i)[0:n, :], ACT.Square,
                                     accum_out=ssum[0:n, i:i + 1]).then_inc(sq_done, 1)
                act.wait_ge(sq_done, i + 1)
                nc.scalar.activation(root[0:n, i:i + 1], ssum[0:n, i:i + 1], ACT.Sqrt, scale=1.0 / D,
                                     bias=eps[0:n, 0:1]).then_inc(root_done, 1)

            for i in range(3):
                root_mean_square(i)
            z_evacuate(0)
            hi_weights(0, 0)
            z_evacuate(1)
            z_evacuate(2)
            root_mean_square(3)
            root_mean_square(4)
            hi_weights(1, 1)
            for i in range(5, XT):
                root_mean_square(i)
                z_evacuate(i - 2)
            z_evacuate(XT - 2)
            z_evacuate(XT - 1)
            act.wait_ge(cst_t, 1)
            nc.scalar.activation(cst[:, :, :], spare[0][:, 0:K * CONSTS].rearrange("p (k i) -> p k i", k=K), ACT.Copy)\
                .then_inc(cst_ready, 1)

            def gate_b(j):
                act.wait_ge(chunk_done, (j + 1) * len(PH1) * CHUNKS)
                act.wait_ge(cb_step, 5 * j + 5)
                act.wait_ge(tail_ready, 2 * j + 2)
                nc.scalar.activation(chunked(t2[:, 0:TOK], CW), item_psum(1, CW), ACT.Sigmoid).then_inc(bsig_ready, 1)
                act.wait_ge(yb_step, 3 * j + 3)
                nc.scalar.activation(at(y_hi, j), t1[:, 0:TOK], ACT.Copy).then_inc(yhi_ready, 1)

            def tails_out(j):
                act.wait_ge(tail_t, j + 1)
                act.wait_ge(state_stored, 32 + 64 * j)
                nc.scalar.activation(tail_out[:, :], spare[1][0:TAIL, 0:P], ACT.Copy).then_inc(tail_rows, 1)

            def phase1_act(j):
                n0 = j * len(PH1)
                first = isinstance(j, int) and j == 0
                end = [item_end(n0 + s) for s in range(len(PH1))]
                if not first:
                    hi_weights(n0 + 1, 1)
                    gate_b(j - 1)
                hi_weights(n0 + 2, 0)
                act.wait_ge(chunk_done, end[0])
                wait(act, ylo_ready, j)
                nc.scalar.activation(chunked(t1[:, :], CWM), item_psum(0, CWM), ACT.Sigmoid).then_inc(glu_ready, 1)
                if not first:
                    tails_out(j - 1)
                hi_weights(n0 + 3, 1)
                act.wait_ge(st_t, 2 * j + 2)
                wait(act, samp_step, 3 * j)
                wait(act, cb_step, 5 * j)
                st = spare[0][:, 0:2 * P].rearrange("p (h m) -> p h m", h=2)
                nc.scalar.activation(sa[:, :, 0:BUF_A].rearrange("p (h b) r -> p h b r", h=2),
                                     st[:, :, 0:4 * BUF_A].rearrange("p h (b r) -> p h b r", b=4), ACT.Copy)\
                    .then_inc(sa_in, 1)
                nc.scalar.activation(sbw[:, :, 0:BUF_B].rearrange("p (h b) r -> p h b r", h=2),
                                     st[:, :, 4 * BUF_A:P].rearrange("p h (b r) -> p h b r", b=4), ACT.Copy)\
                    .then_inc(sb_in, 1)
                hi_weights(n0 + 4, 0)
                act.wait_ge(chunk_done, end[2])
                wait(act, yb_step, 3 * j)
                nc.scalar.activation(chunked(t2[:, 0:CHUNKS * CWB], CWB), item_psum(0, CWB), ACT.Copy).then_inc(bh_ready, 1)
                act.wait_ge(ua_ready, j + 1)
                nc.scalar.activation(sa[:, :, BUF_A:TAPS_A], ua[:, UA_S:UA_S + DEC].unsqueeze(2), ACT.Copy)\
                    .then_inc(sa_in, 1)
                wait(act, tail_t, j)
                nc.scalar.activation(tail_in[:, 0:TAIL_A], ua[:, SEQ:SEQ + TAIL_A], ACT.Copy).then_inc(tail_ready, 1)
                hi_weights(n0 + 5, 1)
                hi_weights(n0 + 6, 0)
                act.wait_ge(ub_ready, j + 1)
                nc.scalar.activation(sbw[:, :, BUF_B:TAPS_B], t2[:, UB_S:UB_S + DEC].unsqueeze(2), ACT.Copy)\
                    .then_inc(sb_in, 1)
                nc.scalar.activation(tail_in[:, TAIL_A:TAIL], t2[:, UB_S - BUF_B:UB_S + DEC], ACT.Copy)\
                    .then_inc(tail_ready, 1)

            phase1_act(0)
            with act.Fori(1, K) as j:
                phase1_act(j)

            def sigmoid_mb(j):
                act.wait_ge(chunk_done, item_end(I2 + 2 * j))
                if not isinstance(j, int) or j:
                    act.wait_ge(mbp_ready, j)
                nc.scalar.activation(chunked(t1[:, 0:TOK], CW), item_psum(0, CW), ACT.Sigmoid).then_inc(mb_ready, 1)

            def phase2_act(j):
                hi_weights(I2 + 1 + 2 * j, 1)
                hi_weights(I2 + 2 + 2 * j, 0)
                sigmoid_mb(j)

            def row_of(chunk):
                return ua[:, CW * chunk:CW * (chunk + 1)]

            def stat_bank(chunk):
                return spare[chunk % 2][:, 0:CW]

            def squares(j0, j1):
                for j in range(j0, j1):
                    act.wait_ge(sub_done, j + 1)
                    wait(act, sqacc_step, j)
                    nc.scalar.activation(sq[:, :], c[:, j, :], ACT.Square).then_inc(sqr_ready, 1)

            hi_weights(I2 + 1, 1)
            gate_b(K - 1)
            hi_weights(I2 + 2, 0)
            act.wait_ge(ylo_ready, K)
            tails_out(K - 1)
            sigmoid_mb(0)
            phase2_act(1)
            for ch in range(CHUNKS):
                act.wait_ge(mean_t, ch + 1)
                nc.scalar.activation(row_of(ch), stat_bank(ch), ACT.Copy).then_inc(mean_ready, 1)
            hi_weights(I2 + 5, 1)
            squares(0, 2)
            hi_weights(I2 + 6, 0)
            sigmoid_mb(2)
            squares(2, 5)
            hi_weights(I2 + 7, 1)
            squares(5, K)
            hi_weights(I2 + 8, 0)
            sigmoid_mb(3)
            for ch in range(CHUNKS):
                act.wait_ge(var_t, ch + 1)
                nc.scalar.activation(row_of(ch), stat_bank(ch), ACT.Sqrt, bias=eps[:, 1:2]).then_inc(std_ready, 1)
            phase2_act(4)
            with act.Fori(5, K) as j:
                phase2_act(j)

            def gate_m(j):
                act.wait_ge(chunk_done, item_end(I3 + 2 * j + 1))
                act.wait_ge(ya_step, 4 * j + 4)
                nc.scalar.activation(chunked(at(c, j), CW), item_psum(1, CW), ACT.Sigmoid).then_inc(ma_ready, 1)

            def phase3_act(j):
                n0 = I3 + 2 * j
                first = isinstance(j, int) and j == 0
                hi_weights(n0 + 1, 1)
                if first:
                    act.wait_ge(mbp_ready, K)
                    act.wait_ge(spilled, 16 * K)
                    act.wait_ge(ln_done, K)
                else:
                    gate_m(j - 1)
                    act.wait_ge(alo_ready, j)
                nc.scalar.activation(t2[:, 0:TOK], at(c, j), ACT.Sigmoid, scale=const(j, C_LNG),
                                     bias=const(j, C_LNB)).then_inc(nsig_ready, 1)
                hi_weights(n0 + 2, 0)
                act.wait_ge(chunk_done, item_end(n0))
                nc.scalar.activation(chunked(t1[:, 0:TOK], CW), item_psum(0, CW), ACT.Sigmoid).then_inc(asig_ready, 1)
                act.wait_ge(ya_step, 4 * j + 4)
                nc.scalar.activation(at(y_hi, j), t2[:, 0:TOK], ACT.Copy).then_inc(ahi_ready, 1)

            phase3_act(0)
            with act.Fori(1, K) as j:
                phase3_act(j)

            def hi_out_rows(q, s, m):
                act.wait_ge(raw_in[s], (q - s) * 8 + 16)
                act.wait_ge(chunk_done, item_end(I4 - 1))
                nc.scalar.activation(at(w_out_hi, m), raw[:, s, :, :].rearrange("p k e -> p (k e)"), ACT.Copy)\
                    .then_inc(hi_ready, 1)

            def hi_pa(q, ring, item):
                act.wait_ge(raw_in[1], (q - 1) * 8 + 16)
                act.wait_ge(chunk_done, item_end(item - 2))
                nc.scalar.activation(w_hi[:, ring, :, :], raw[:, 1, :, :], ACT.Copy).then_inc(hi_ready, 1)

            hi_weights(I4 + 1, 1)
            gate_m(K - 1)
            with act.Fori(0, (K - 2) // 2) as jj:
                for r in range(2):
                    hi_out_rows(I4 + 2 + 2 * r + 4 * jj, 0, 2 * jj + r)
                    hi_pa(I4 + 3 + 2 * r + 4 * jj, r, I4 + 2 + r + 2 * jj)
            hi_out_rows(I4 + 2 * K - 2, 0, K - 2)
            hi_out_rows(I4 + 2 * K - 1, 1, K - 1)

            def hi_merged(i, s, n=P):
                if isinstance(i, int) and i < 2:
                    act.wait_ge(chunk_done, item_end(I4 + K - 2 + i))
                    act.wait_ge(merged_done, CHUNKS * (K - 1) + 1)
                else:
                    act.wait_ge(out_mm, i - 1)
                    act.wait_ge(merged_done, CHUNKS * K)
                cols = slice(P * i, P * i + n) if isinstance(i, int) else bass.ds(P * i, n)
                nc.scalar.activation(w_hi[:, s, :, 0:n], c[:, :, cols], ACT.Copy).then_inc(hi_ready, 1)

            def final_norm(i, s, n=P):
                col = slice(i, i + 1) if isinstance(i, int) else bass.ds(i, 1)
                t = (t1, t2)[s]
                act.wait_ge(h_ready, i + 1)
                act.wait_ge(hsq_done, i) if not isinstance(i, int) or i else None
                a, b = ssum[0:n, col], root[0:n, col]
                nc.scalar.activation(sq[0:n, 0:D], t[0:n, 0:D], ACT.Square, accum_out=a).then_inc(hsq_done, 1)
                act.wait_ge(hsq_done, i + 1)
                nc.scalar.activation(b, a, ACT.Sqrt, scale=1.0 / D, bias=eps[0:n, 0:1]).then_inc(hroot_done, 1)

            hi_merged(0, 0)
            hi_merged(1, 1)
            final_norm(0, 0)
            hi_merged(2, 0)
            final_norm(1, 1)
            with act.Fori(1, (TT - 1) // 2 - 1) as ii:
                hi_merged(2 * ii + 1, 1)
                final_norm(2 * ii, 0)
                hi_merged(2 * ii + 2, 0)
                final_norm(2 * ii + 1, 1)
            hi_merged(TT - 2, 1)
            final_norm(TT - 3, 0)
            hi_merged(TT - 1, 0, DEC)
            final_norm(TT - 2, 1)
            act.wait_ge(h_ready, TT + 1)
            final_norm(TT - 1, 0, DEC)

        @block.vector
        def _(dve):
            V = nc.vector
            dve.wait_ge(gin_in, 16)

            def z_low(i):
                n = x_rows(i)
                for h in range(2):
                    dve.wait_ge(zhi_done, 2 * i + h + 1)
                    src = x_bank(i, h).rearrange("p (k t) -> p k t", k=4)[:, :, 0:n]
                    V.tensor_tensor(z_lo[:, 4 * h:4 * h + 4, P * i:P * i + n], src,
                                    f(z_hi[:, 4 * h:4 * h + 4, P * i:P * i + n]), ALU.subtract).then_inc(zlo_done, 1)


            def normalize(i):
                n = x_rows(i)
                dve.wait_ge(root_done, i + 2)
                V.reciprocal(rinv[0:n, i:i + 1], root[0:n, i:i + 1]).then_inc(rinv_done, 1)
                dve.wait_ge(rinv_done, i + 1)
                V.scalar_tensor_tensor(out=x_slot(i)[0:n, :], in0=x_slot(i)[0:n, :], scalar=rinv[0:n, i:i + 1],
                                       in1=gin[0:n, :], op0=ALU.mult, op1=ALU.mult).then_inc(xn_ready, 1)

            for i in range(3):
                normalize(i)
            for i in range(3):
                z_low(i)
            normalize(3)
            normalize(4)
            for i in range(5, XT):
                normalize(i)
                z_low(i - 2)
            z_low(XT - 2)
            z_low(XT - 1)
            dve.wait_ge(cst_ready, 1)

            def conv_a(j, op0, op1):
                def cj(start, n, step=1):
                    cols = slice(start, start + step * (n - 1) + 1, step)
                    return c[:, j, cols] if isinstance(j, int) else \
                        c[:, bass.ds(j, 1), cols].rearrange("p a n -> p (a n)")

                def u(start, n):
                    return ua[:, start:start + 2 * n - 1:2]

                def done(op):
                    dve.wait_ge(conv_step, j * CONV_OPS + (op + 1))

                a_out, b_out = sq[:, 0:HALF + 1], sq[:, HALF + 1:2 * HALF + 1]
                even, odd = cj(0, HALF, 2), cj(1, HALF, 2)
                for op in range(op0, op1):
                    if op == 0:
                        ins = V.tensor_scalar(cj(0, SEQ), ua[:, BUF_A:BUF_A + SEQ], const(j, BUF_A), const(j, C_BIAS),
                                              ALU.mult, ALU.add)
                    elif op < OP_S:
                        i, odd_taps = divmod(op - OP_AB, 2)
                        out = b_out if odd_taps else a_out
                        src = u(2 * i + odd_taps, HALF if odd_taps else HALF + 1)
                        tap = const(j, 2 * i + odd_taps)
                        if i == 0:
                            ins = V.tensor_scalar(out, src, tap, None, ALU.mult)
                        else:
                            done(op - 2)
                            ins = V.scalar_tensor_tensor(out=out, in0=src, scalar=tap, in1=out,
                                                         op0=ALU.mult, op1=ALU.add)
                    elif op == OP_S:
                        n = HALF + PAIRS - 1
                        done(OP_S - 1)
                        dve.wait_ge(tail_ready, 2 * j + 1)
                        ins = V.tensor_tensor(u(1, n), u(1, n), u(2, n), ALU.add)
                    elif op < OP_END:
                        i, h = divmod(op - OP_C, 2)
                        done(OP_S if i == 0 else op - 2)
                        dst = cj(1 + h * HALF, HALF // 2, 2)
                        tap = tap_sum[:, j, i:i + 1] if isinstance(j, int) else \
                            tap_sum[:, bass.ds(j, 1), i:i + 1].rearrange("p a n -> p (a n)")
                        ins = V.scalar_tensor_tensor(out=dst, in0=u(1 + 2 * i + h * HALF, HALF // 2), scalar=tap,
                                                     in1=dst, op0=ALU.mult, op1=ALU.add)
                    elif op == OP_END:
                        ins = V.tensor_tensor(even, even, a_out[:, 0:HALF], ALU.add)
                    elif op == OP_END + 1:
                        done(OP_END - 1)
                        ins = V.tensor_tensor(odd, odd, a_out[:, 1:HALF + 1], ALU.subtract)
                    elif op == OP_END + 2:
                        done(OP_END)
                        ins = V.tensor_tensor(even, even, b_out, ALU.add)
                    elif op == OP_END + 3:
                        done(OP_END + 1)
                        ins = V.tensor_tensor(odd, odd, b_out, ALU.subtract)
                    else:
                        ins = V.memset(ua[:, 0:LEAD], 0.0)
                    ins.then_inc(conv_step, 1)

            SPLIT = [0, 9, 21, 25, 36, 48, CONV_OPS]
            V.tensor_tensor(tap_sum[:, :, :], cst[:, :, 0:BUF_A:2], cst[:, :, 1:BUF_A:2], ALU.add).then_inc(taps_ready, 1)
            dve.wait_ge(taps_ready, 1)

            def lo_weights(q, s):
                if isinstance(q, int) and q > I2:
                    return
                dve.wait_ge(hi_ready, q + 1)
                V.tensor_tensor(w_lo[:, s, :, :], raw[:, s, :, :], f(w_hi[:, s, :, :]), ALU.subtract)\
                    .then_inc(lo_ready, 1)

            def sample_a(j):
                dst = c[:, j, SEQ:TOK] if isinstance(j, int) else \
                    c[:, bass.ds(j, 1), SEQ:TOK].rearrange("p a n -> p (a n)")
                dve.wait_ge(sa_in, 2 * j + 2)
                w = const(j, 0, TAPS_A).unsqueeze(1).broadcast_to([P, DEC, TAPS_A])
                V.tensor_tensor(sa[:, :, :], sa[:, :, :], w, ALU.mult).then_inc(samp_step, 1)
                dve.wait_ge(samp_step, 3 * j + 1)
                V.tensor_reduce(dst, sa[:, :, :], mybir.AxisListType.X, ALU.add).then_inc(samp_step, 1)
                dve.wait_ge(samp_step, 3 * j + 2)
                V.tensor_scalar(dst, dst, const(j, C_BIAS), None, ALU.add).then_inc(samp_step, 1)

            def finish_b(j):
                n0 = (j + 1) * len(PH1)
                lo_weights(n0 + 1, 1)
                dve.wait_ge(bsig_ready, j + 1)
                dve.wait_ge(yb_step, 3 * j + 1)
                V.tensor_tensor(chunked(t1[:, 0:TOK], CW), item_psum(1, CW), chunked(t1[:, 0:TOK], CW), ALU.mult)\
                    .then_inc(yb_step, 1)
                dve.wait_ge(yb_step, 3 * j + 2)
                V.tensor_tensor(t1[:, 0:TOK], t1[:, 0:TOK], t2[:, 0:TOK], ALU.mult).then_inc(yb_step, 1)
                conv_a(j, SPLIT[4], SPLIT[5])
                dve.wait_ge(yhi_ready, j + 1)
                V.tensor_tensor(at(y_lo, j), t1[:, 0:TOK], f(at(y_hi, j)), ALU.subtract).then_inc(ylo_ready, 1)
                lo_weights(n0 + 2, 0)
                conv_a(j, SPLIT[5], SPLIT[6])

            def phase1_dve(j):
                n0 = j * len(PH1)
                first = isinstance(j, int) and j == 0
                if first:
                    lo_weights(2, 0)
                else:
                    finish_b(j - 1)
                dve.wait_ge(chunk_done, item_end(n0 + 1))
                dve.wait_ge(glu_ready, j + 1)
                wait(dve, conv_step, j * CONV_OPS)
                wait(dve, tail_ready, 2 * j)
                V.tensor_tensor(chunked(ua[:, LEAD:LEAD + ZT], CWM), item_psum(1, CWM), chunked(t1[:, :], CWM),
                                ALU.mult).then_inc(ua_ready, 1)
                lo_weights(n0 + 3, 1)
                dve.wait_ge(ua_ready, j + 1)
                conv_a(j, SPLIT[0], SPLIT[1])
                sample_a(j)
                lo_weights(n0 + 4, 0)
                conv_a(j, SPLIT[1], SPLIT[2])
                dve.wait_ge(chunk_done, item_end(n0 + 3))
                dve.wait_ge(bh_ready, j + 1)
                ub = chunked(t2[:, 0:CHUNKS * CWB], CWB)
                V.tensor_tensor(ub, item_psum(1, CWB), ub, ALU.mult).then_inc(ub_ready, 1)
                lo_weights(n0 + 5, 1)
                dve.wait_ge(ub_ready, j + 1)
                lead = META - BUF_B - SKIP
                V.tensor_scalar(t1[:, 0:SEQ], t2[:, lead:lead + SEQ], const(j, C_TB), None, ALU.mult)\
                    .then_inc(cb_step, 1)
                for k in range(1, TAPS_B):
                    dve.wait_ge(cb_step, 5 * j + k)
                    V.scalar_tensor_tensor(out=t1[:, 0:SEQ], in0=t2[:, lead + k:lead + k + SEQ],
                                           scalar=const(j, C_TB + k), in1=t1[:, 0:SEQ],
                                           op0=ALU.mult, op1=ALU.add).then_inc(cb_step, 1)
                conv_a(j, SPLIT[2], SPLIT[3])
                dve.wait_ge(sb_in, 2 * j + 2)
                w = const(j, C_TB, TAPS_B).unsqueeze(1).broadcast_to([P, DEC, TAPS_B])
                V.tensor_tensor(sbw[:, :, :], sbw[:, :, :], w, ALU.mult).then_inc(cb_step, 1)
                dve.wait_ge(cb_step, 5 * j + 4)
                V.tensor_reduce(t1[:, SEQ:TOK], sbw[:, :, :], mybir.AxisListType.X, ALU.add).then_inc(cb_step, 1)
                dve.wait_ge(cb_step, 5 * j + 5)
                dve.wait_ge(chunk_done, item_end(n0 + 4))
                V.tensor_tensor(chunked(t1[:, 0:TOK], CW), item_psum(0, CW), chunked(t1[:, 0:TOK], CW), ALU.mult)\
                    .then_inc(yb_step, 1)
                lo_weights(n0 + 6, 0)
                conv_a(j, SPLIT[3], SPLIT[4])

            phase1_dve(0)
            with dve.Fori(1, K) as j:
                phase1_dve(j)
            finish_b(K - 1)

            def merge_b(j):
                dve.wait_ge(chunk_done, item_end(I2 + 2 * j + 1))
                dve.wait_ge(mb_ready, j + 1)
                if isinstance(j, int) and j == 0:
                    dve.wait_ge(yb_step, 3 * K)
                else:
                    dve.wait_ge(spilled, 16 * j)
                V.tensor_tensor(chunked(t2[:, 0:TOK], CW), item_psum(1, CW), chunked(t1[:, 0:TOK], CW), ALU.mult)\
                    .then_inc(mbp_ready, 1)

            row = ua[:, 0:TOK]
            dve.wait_ge(conv_step, K * CONV_OPS)
            dve.wait_ge(samp_step, 3 * K)
            dve.wait_ge(tail_ready, 2 * K)
            V.tensor_tensor(row, c[:, 0, :], c[:, 1, :], ALU.add).then_inc(sum_step, 1)
            for j in range(2, K):
                dve.wait_ge(sum_step, j - 1)
                V.tensor_tensor(row, row, c[:, j, :], ALU.add).then_inc(sum_step, 1)
            merge_b(0)
            merge_b(1)
            dve.wait_ge(mean_ready, CHUNKS)
            for j in range(K):
                V.tensor_tensor(c[:, j, :], c[:, j, :], row, ALU.subtract).then_inc(sub_done, 1)
            dve.wait_ge(sub_done, K)
            for j in range(K):
                dve.wait_ge(sqr_ready, j + 1)
                if j == 0:
                    V.tensor_copy(row, sq[:, :]).then_inc(sqacc_step, 1)
                else:
                    dve.wait_ge(sqacc_step, j)
                    V.tensor_tensor(row, row, sq[:, :], ALU.add).then_inc(sqacc_step, 1)
                if j == 4:
                    merge_b(2)
            merge_b(3)
            dve.wait_ge(std_ready, CHUNKS)
            V.reciprocal(row, row).then_inc(rstd_ready, 1)
            dve.wait_ge(rstd_ready, 1)
            for j in range(K):
                V.tensor_tensor(c[:, j, :], c[:, j, :], row, ALU.mult).then_inc(ln_done, 1)
            with dve.Fori(4, K) as j:
                merge_b(j)

            def phase3_dve(j):
                dve.wait_ge(nsig_ready, j + 1)
                V.tensor_scalar(at(c, j), at(c, j), const(j, C_LNG), const(j, C_LNB), ALU.mult, ALU.add)\
                    .then_inc(ya_step, 1)
                dve.wait_ge(ya_step, 4 * j + 1)
                V.tensor_tensor(t2[:, 0:TOK], t2[:, 0:TOK], at(c, j), ALU.mult).then_inc(ya_step, 1)
                dve.wait_ge(ya_step, 4 * j + 2)
                dve.wait_ge(asig_ready, j + 1)
                V.tensor_tensor(chunked(t2[:, 0:TOK], CW), item_psum(0, CW), chunked(t2[:, 0:TOK], CW), ALU.mult)\
                    .then_inc(ya_step, 1)
                dve.wait_ge(ya_step, 4 * j + 3)
                V.tensor_tensor(t2[:, 0:TOK], t2[:, 0:TOK], t1[:, 0:TOK], ALU.mult).then_inc(ya_step, 1)
                dve.wait_ge(ahi_ready, j + 1)
                V.tensor_tensor(at(y_lo, j), t2[:, 0:TOK], f(at(y_hi, j)), ALU.subtract).then_inc(alo_ready, 1)

            dve.wait_ge(ln_done, K)
            with dve.Fori(0, K) as j:
                phase3_dve(j)

            dve.wait_ge(ma_ready, K)

            def merge_a(j, s):
                dve.wait_ge(mb_back[s], (j - s) * 8 + 16)
                for ch in range(CHUNKS):
                    dst = c[:, j, CW * ch:CW * (ch + 1)] if isinstance(j, int) else \
                        c[:, bass.ds(j, 1), CW * ch:CW * (ch + 1)].rearrange("p a n -> p (a n)")
                    dve.wait_ge(chunk_done, (j + I4) * CHUNKS + (ch + 1))
                    V.tensor_tensor(dst, ps[s][:, ch, 0:CW], dst, ALU.mult).then_inc(mul_done, 1)
                    dve.wait_ge(mul_done, j * CHUNKS + (ch + 1))
                    V.tensor_tensor(dst, dst, (t1, t2)[s][:, CW * ch:CW * (ch + 1)], ALU.add).then_inc(merged_done, 1)

            with dve.Fori(0, K // 2) as jj:
                for s in range(2):
                    merge_a(2 * jj + s, s)

            dve.wait_ge(gf_in, 16)

            def residual(i, s, n=P):
                t = (t1, t2)[s]
                dve.wait_ge(out_mm, i + 1)
                dve.wait_ge(xr_in[s], (i - s) * 8 + 16)
                tv = t[0:n, 0:D].rearrange("p (h e) -> p h e", h=2)
                V.tensor_tensor(tv, ps[s][0:n, 0:2, :], tv, ALU.add).then_inc(h_ready, 1)

            def scale_rows(i, s, n=P):
                t = (t1, t2)[s]
                col = slice(i, i + 1) if isinstance(i, int) else bass.ds(i, 1)
                a, b = root[0:n, col], rinv[0:n, col]
                dve.wait_ge(hroot_done, i + 1)
                V.reciprocal(b, a).then_inc(hinv_done, 1)
                dve.wait_ge(hinv_done, i + 1)
                V.scalar_tensor_tensor(out=t[0:n, 0:D], in0=t[0:n, 0:D], scalar=b, in1=gfin[0:n, :],
                                       op0=ALU.mult, op1=ALU.mult).then_inc(y_ready, 1)

            with dve.Fori(0, (TT - 1) // 2) as ii:
                for s in range(2):
                    residual(2 * ii + s, s)
                    scale_rows(2 * ii + s, s)
            dve.wait_ge(xr_in[0], (TT - 1) * 8 + 16)
            for h in range(2):
                half = t1[0:DEC, h * 512:(h + 1) * 512]
                dve.wait_ge(out_mm, TT + h)
                V.tensor_tensor(half, ps[0][0:DEC, h, :], half, ALU.add).then_inc(half_added, 1)
                dve.wait_ge(half_added, h + 1)
                V.tensor_tensor(half, ps[0][QUAD:QUAD + DEC, h, :], half, ALU.add).then_inc(h_ready, 1)
            scale_rows(TT - 1, 0, DEC)

        @block.tensor
        def _(pe):
            def chunk(s, hi, lo, off, width, ch, k0=0, k1=K):
                lo_col, hi_col = off + ch * width, off + (ch + 1) * width
                for k in range(k0, k1):
                    parts = ((w_hi, hi), (w_hi, lo), (w_lo, hi))
                    for n, (w, x) in enumerate(parts):
                        last = nc.tensor.matmul(ps[s][:, ch, 0:width], w[:, s, k, :], x[:, k, lo_col:hi_col],
                                                start=(k == 0 and n == 0), stop=(k == K - 1 and n == 2))
                if k1 == K:
                    last.then_inc(chunk_done, 1)

            def item(s, hi, lo, off, width):
                for ch in range(CHUNKS):
                    chunk(s, hi, lo, off, width, ch)

            def transpose_x(i):
                n = x_rows(i)
                pe.wait_ge(xn_ready, i + 1)
                for h in range(2):
                    wait(pe, zlo_done, 2 * i + h - 3)
                    for k in range(4):
                        col = (4 * h + k) * P
                        last = nc.tensor.transpose(x_bank(i, h)[:, k * P:k * P + n], x_slot(i)[0:n, col:col + P],
                                                   ident[0:n, 0:n])
                    last.then_inc(xt_done, 1)

            pe.wait_ge(pool_const, 3)
            for i in range(3):
                transpose_x(i)

            def first_chunk(s, ch, between):
                chunk(s, z_hi, z_lo, 0, CWM, ch, 0, K // 2)
                if between:
                    transpose_x(between[0])
                chunk(s, z_hi, z_lo, 0, CWM, ch, K // 2, K)
                if between[1:]:
                    transpose_x(between[1])

            pe.wait_ge(zlo_done, 5)
            pe.wait_ge(lo_ready, 1)
            chunk(0, z_hi, z_lo, 0, CWM, 0, 0, K // 2)
            transpose_x(3)
            pe.wait_ge(zlo_done, 6)
            chunk(0, z_hi, z_lo, 0, CWM, 0, K // 2, K)
            transpose_x(4)
            pe.wait_ge(lo_ready, 2)
            first_chunk(1, 0, [5, 6])
            pe.wait_ge(zlo_done, 12)
            first_chunk(0, 1, [7, 8])
            pe.wait_ge(zlo_done, 16)
            first_chunk(1, 1, [])
            pe.wait_ge(zlo_done, 2 * XT)
            pe.wait_ge(pool_const, 6)
            pe.wait_ge(cst_in, 80)
            for k in range(K):
                last = nc.tensor.transpose(spare[0][:, k * CONSTS:(k + 1) * CONSTS], sq[0:CONSTS, k * P:(k + 1) * P],
                                           ident[0:CONSTS, 0:CONSTS])
            last.then_inc(cst_t, 1)
            chunk(0, z_hi, z_lo, 0, CWM, 2)
            chunk(1, z_hi, z_lo, 0, CWM, 2)

            def await_tails(j):
                pe.wait_ge(tail_ready, 2 * j + 2)

            def transpose_tails():
                nc.tensor.transpose(spare[1][0:TAIL, 0:P], tail_in[:, :], ident[:, :]).then_inc(tail_t, 1)

            def transpose_states(j):
                pe.wait_ge(st_in, 32 * j + 32)
                if isinstance(j, int) and j == 0:
                    pe.wait_ge(cst_ready, 1)
                else:
                    pe.wait_ge(sb_in, 2 * j - 1)
                for h in range(2):
                    nc.tensor.transpose(spare[0][:, h * P:(h + 1) * P], st_raw[:, h, :], ident[:, :]).then_inc(st_t, 1)

            def phase1_pe(j):
                n0 = j * len(PH1)
                first = isinstance(j, int) and j == 0
                freed = [(yb_step, 3 * j - 2), (yb_step, 3 * j - 1), (glu_ready, j + 1), (ua_ready, j + 1),
                         (bh_ready, j + 1), (ub_ready, j + 1)]
                for s, (_, off, width) in enumerate(PH1):
                    if s == (2 if first else 0):
                        transpose_states(j)
                    if s == 1 and not first:
                        await_tails(j - 1)
                    if first and s < 2:
                        continue
                    pe.wait_ge(lo_ready, n0 + s + 1)
                    pe.wait_ge(*freed[s])
                    item(s % 2, z_hi, z_lo, off, width)
                    if s == 1 and not first:
                        transpose_tails()

            phase1_pe(0)
            with pe.Fori(1, K) as j:
                phase1_pe(j)

            def phase2_pe(j):
                n0 = I2 + 2 * j
                first = isinstance(j, int) and j == 0
                pe.wait_ge(lo_ready, n0 + 1)
                pe.wait_ge(*((yb_step, 3 * K - 2) if first else (mb_ready, j)))
                item(0, z_hi, z_lo, META, CW)
                if first:
                    await_tails(K - 1)
                    transpose_tails()
                    pe.wait_ge(ylo_ready, K)
                pe.wait_ge(lo_ready, n0 + 2)
                pe.wait_ge(*((yb_step, 3 * K - 1) if first else (mbp_ready, j)))
                item(1, y_hi, y_lo, 0, CW)

            def column_means(ready, value, left, done):
                pe.wait_ge(ready, value)
                for ch in range(CHUNKS):
                    if ch == 2:
                        pe.wait_ge(left, 1)
                    nc.tensor.matmul(spare[ch % 2][:, 0:CW], ident[:, :], ua[:, CW * ch:CW * (ch + 1)],
                                     start=True, stop=True).then_inc(done, 1)

            phase2_pe(0)
            phase2_pe(1)
            pe.wait_ge(pool_const, 7)
            pe.wait_ge(tail_rows, K)
            column_means(sum_step, K - 1, mean_ready, mean_t)
            phase2_pe(2)
            phase2_pe(3)
            column_means(sqacc_step, K, std_ready, var_t)
            with pe.Fori(4, K) as j:
                phase2_pe(j)

            def phase3_pe(j):
                n0 = I3 + 2 * j
                first = isinstance(j, int) and j == 0
                pe.wait_ge(lo_ready, n0 + 1)
                pe.wait_ge(*((mb_ready, K) if first else (ya_step, 4 * j - 1)))
                item(0, z_hi, z_lo, META, CW)
                pe.wait_ge(lo_ready, n0 + 2)
                pe.wait_ge(*((mbp_ready, K) if first else (ma_ready, j)))
                item(1, z_hi, z_lo, META, CW)

            phase3_pe(0)
            with pe.Fori(1, K) as j:
                phase3_pe(j)

            pe.wait_ge(alo_ready, K)

            def phase4_pe(j, s, split):
                pe.wait_ge(lo_ready, split + 1)
                if isinstance(j, int) and j < 2:
                    pe.wait_ge(*((ya_step, 4 * K - 1), (ma_ready, K))[j])
                else:
                    pe.wait_ge(mul_done, j * CHUNKS - CHUNKS)
                item(s, y_hi, y_lo, 0, CW)

            phase4_pe(0, 0, I4)
            phase4_pe(1, 1, I4 + 1)
            with pe.Fori(1, K // 2) as jj:
                for s in range(2):
                    phase4_pe(2 * jj + s, s, I4 + 4 * jj + 2 * s - 1)

            def out_tile(i, s, n=P):
                pe.wait_ge(lo_ready, i + (I4 + 2 * K + 1))
                if isinstance(i, int) and i < 2:
                    pe.wait_ge(mul_done, CHUNKS * (K - 1 + i))
                else:
                    pe.wait_ge(h_ready, i - 1)
                for h in range(2):
                    for k in range(K):
                        parts = ((w_hi, w_out_hi), (w_hi, w_out_lo), (w_lo, w_out_hi))
                        for m, (x, w) in enumerate(parts):
                            last = nc.tensor.matmul(ps[s][0:n, h, :], x[:, s, k, 0:n], w[:, k, h * 512:(h + 1) * 512],
                                                    start=(k == 0 and m == 0), stop=(k == K - 1 and m == 2))
                last.then_inc(out_mm, 1)

            out_tile(0, 0)
            out_tile(1, 1)
            with pe.Fori(1, (TT - 1) // 2) as ii:
                for s in range(2):
                    out_tile(2 * ii + s, s)
            pe.wait_ge(lo_ready, TT + (I4 + 2 * K))
            pe.wait_ge(h_ready, TT - 2)
            for h in range(2):
                for k in range(K):
                    for m, w in enumerate((w_out_hi, w_out_lo)):
                        last = nc.tensor.matmul(ps[0][0:QUAD + DEC, h, :], w_hi[:, 0, k, 0:QUAD + DEC],
                                                w[:, k, h * 512:(h + 1) * 512],
                                                start=(k == 0 and m == 0), stop=(k == K - 1 and m == 1))
                last.then_inc(out_mm, 1)


_INS = ["x_prompt", "x_sample", "state_conv_a", "state_conv_b", "meta_tokens", "norm_g", "w_in", "conv_a_w",
        "conv_a_b", "ln_a_g", "ln_a_b", "conv_b_w", "w_pa", "w_pb", "w_out", "final_norm_g"]
_OUTS = [(1, 1024, 1024), (8, 1, 1024), (1, 1, 30, 1024), (1, 1, 2, 1024), (1, 8, 30, 1024), (1, 8, 2, 1024)]


def kernel(**inputs):
    import numpy as _np
    import concourse.bacc as _bacc
    from concourse import mybir as _mybir
    from concourse.bass_utils import run_bass_kernel_spmd as _run

    nc = _bacc.Bacc("TRN2", target_bir_lowering=False, num_devices=1)
    arrays, args = {}, []
    for name in _INS:
        a = _np.ascontiguousarray(inputs[name])
        arrays[f"in_{name}_dram"] = a
        args.append(nc.dram_tensor(f"in_{name}_dram", a.shape, _mybir.dt.from_np(a.dtype), kind="ExternalInput").ap())
    for i, shape in enumerate(_OUTS):
        args.append(nc.dram_tensor(f"out_{i}_dram", shape, _mybir.dt.float32, kind="ExternalOutput").ap())
    decoder_step(nc, *args)
    r = _run(nc, [arrays], core_ids=[0])
    return tuple(r.results[0][f"out_{i}_dram"] for i in range(len(_OUTS)))
```
